# Optimizing a Trainium2 kernel written in Bass

```python
import jax, jax.numpy as jnp
from jax import lax
import numpy as np

D_MODEL = 1024
BATCH = 1
SEQ = 256
DEPTH = 2

D_FF = 2816
D_MIX = D_MODEL
POOL_CH = D_MIX // 2
POOL_WINDOWS = (2, 4, 8, 16)
POOL_GROUPS = len(POOL_WINDOWS)
POOL_GC = POOL_CH // POOL_GROUPS
CONV_CH = D_MIX - POOL_CH
CONV_WIDTH = 31
AB_IN = POOL_CH + 2 * CONV_CH
SGU_CH = D_MIX
SGU_HEADS = 8
SGU_HC = SGU_CH // SGU_HEADS
CHUNK = 128
N_EVEN = (DEPTH + 1) // 2
N_ODD = DEPTH // 2
EPS = 1e-6

kernel_name = "hybrid_pool_conv_sgu_macaron"

def rms_norm(x, g):
    xf = x.astype(jnp.float32)
    y = xf * lax.rsqrt(jnp.mean(xf * xf, axis=-1, keepdims=True) + EPS)
    return (y * g.astype(jnp.float32)).astype(x.dtype)

def layer_norm(x, g, b):
    xf = x.astype(jnp.float32)
    mu = jnp.mean(xf, axis=-1, keepdims=True)
    var = jnp.mean(jnp.square(xf - mu), axis=-1, keepdims=True)
    y = (xf - mu) * lax.rsqrt(var + EPS)
    return (y * g.astype(jnp.float32) + b.astype(jnp.float32)).astype(x.dtype)

def swiglu_ffn(x, w_in, w_out):
    gate, up = jnp.split(x @ w_in, 2, axis=-1)
    return (jax.nn.silu(gate) * up) @ w_out

def pool_mixer(u, w, b, scale):
    bsz, t_len, _ = u.shape
    csum = jnp.cumsum(u.astype(jnp.float32), axis=1)
    pos = jnp.arange(t_len, dtype=jnp.int32)
    means = []
    for g, win in enumerate(POOL_WINDOWS):
        cg = csum[..., g * POOL_GC:(g + 1) * POOL_GC]
        shifted = jnp.pad(cg[:, :t_len - win], ((0, 0), (win, 0), (0, 0)))
        count = jnp.minimum(pos + 1, win).astype(jnp.float32)[None, :, None]
        means.append((cg - shifted) / count)
    pooled = jnp.concatenate(means, axis=-1).astype(u.dtype) - u
    pooled = pooled.reshape(bsz, t_len, POOL_GROUPS, POOL_GC)
    mixed = jnp.einsum('btgc,gcd->btgd', pooled, w) + b
    return mixed.reshape(bsz, t_len, POOL_CH) * scale

def conv_module(h, conv_w, conv_b, ln_g, ln_b):
    a, gate = jnp.split(h, 2, axis=-1)
    g = a * jax.nn.sigmoid(gate)
    y = lax.conv_general_dilated(
        g, conv_w[:, None, :], window_strides=(1,), padding=((CONV_WIDTH - 1, 0),),
        dimension_numbers=('NWC', 'WIO', 'NWC'), feature_group_count=CONV_CH) + conv_b
    return jax.nn.silu(layer_norm(y, ln_g, ln_b))

def pool_conv_mixer(xn, w_in, pool_w, pool_b, pool_scale, conv_w, conv_b, ln_g, ln_b, w_out):
    h = xn @ w_in
    ya = pool_mixer(h[..., :POOL_CH], pool_w, pool_b, pool_scale)
    yb = conv_module(h[..., POOL_CH:], conv_w, conv_b, ln_g, ln_b)
    return jnp.concatenate([ya, yb], axis=-1) @ w_out

def sgu_mixer(xn, w_in, ln_g, ln_b, w_s, b_s, w_out):
    bsz, t_len, _ = xn.shape
    z = jax.nn.gelu(xn @ w_in, approximate=False)
    u, v = jnp.split(z, 2, axis=-1)
    v = layer_norm(v, ln_g, ln_b)
    v = v.reshape(bsz, t_len // CHUNK, CHUNK, SGU_HEADS, SGU_HC)
    mask = jnp.tril(jnp.ones((CHUNK, CHUNK), dtype=w_s.dtype))
    w_masked = w_s * mask
    v = jnp.einsum('hst,bnthc->bnshc', w_masked, v) + b_s.T[None, None, :, :, None]
    v = v.reshape(bsz, t_len, SGU_CH)
    return (u * v) @ w_out

def setup_inputs(seed: int = 0) -> dict:
    key = jax.random.key(seed)
    ks = iter(jax.random.split(key, 32))

    def nrm(shape, scale):
        return jax.random.normal(next(ks), shape, jnp.float32) * scale

    def gain(shape):
        return 1.0 + nrm(shape, 0.05)

    return {
        "x": nrm((BATCH, SEQ, D_MODEL), 1.0),
        "ffn1_norm": gain((DEPTH, D_MODEL)),
        "ffn1_w_in": nrm((DEPTH, D_MODEL, 2 * D_FF), D_MODEL ** -0.5),
        "ffn1_w_out": nrm((DEPTH, D_FF, D_MODEL), D_FF ** -0.5),
        "mix_norm": gain((DEPTH, D_MODEL)),
        "ffn2_norm": gain((DEPTH, D_MODEL)),
        "ffn2_w_in": nrm((DEPTH, D_MODEL, 2 * D_FF), D_MODEL ** -0.5),
        "ffn2_w_out": nrm((DEPTH, D_FF, D_MODEL), D_FF ** -0.5),
        "ab_w_in": nrm((N_EVEN, D_MODEL, AB_IN), D_MODEL ** -0.5),
        "pool_w": nrm((N_EVEN, POOL_GROUPS, POOL_GC, POOL_GC), POOL_GC ** -0.5),
        "pool_b": nrm((N_EVEN, POOL_GROUPS, POOL_GC), 0.02),
        "pool_scale": 0.5 + nrm((N_EVEN, POOL_CH), 0.05),
        "conv_w": nrm((N_EVEN, CONV_WIDTH, CONV_CH), CONV_WIDTH ** -0.5),
        "conv_b": nrm((N_EVEN, CONV_CH), 0.02),
        "conv_ln_g": gain((N_EVEN, CONV_CH)),
        "conv_ln_b": nrm((N_EVEN, CONV_CH), 0.02),
        "ab_w_out": nrm((N_EVEN, D_MIX, D_MODEL), D_MIX ** -0.5),
        "sgu_w_in": nrm((N_ODD, D_MODEL, 2 * SGU_CH), D_MODEL ** -0.5),
        "sgu_ln_g": gain((N_ODD, SGU_CH)),
        "sgu_ln_b": nrm((N_ODD, SGU_CH), 0.02),
        "sgu_w": nrm((N_ODD, SGU_HEADS, CHUNK, CHUNK), CHUNK ** -0.5),
        "sgu_b": 1.0 + nrm((N_ODD, SGU_HEADS, CHUNK), 0.05),
        "sgu_w_out": nrm((N_ODD, SGU_CH, D_MODEL), SGU_CH ** -0.5),
        "final_norm": gain((D_MODEL,)),
    }

def reference(x, ffn1_norm, ffn1_w_in, ffn1_w_out, mix_norm, ffn2_norm, ffn2_w_in, ffn2_w_out,
              ab_w_in, pool_w, pool_b, pool_scale, conv_w, conv_b, conv_ln_g, conv_ln_b, ab_w_out,
              sgu_w_in, sgu_ln_g, sgu_ln_b, sgu_w, sgu_b, sgu_w_out, final_norm):
    for i in range(DEPTH):
        x = x + 0.5 * swiglu_ffn(rms_norm(x, ffn1_norm[i]), ffn1_w_in[i], ffn1_w_out[i])
        xn = rms_norm(x, mix_norm[i])
        if i % 2 == 0:
            j = i // 2
            y = pool_conv_mixer(xn, ab_w_in[j], pool_w[j], pool_b[j], pool_scale[j],
                                conv_w[j], conv_b[j], conv_ln_g[j], conv_ln_b[j], ab_w_out[j])
        else:
            j = i // 2
            y = sgu_mixer(xn, sgu_w_in[j], sgu_ln_g[j], sgu_ln_b[j], sgu_w[j], sgu_b[j], sgu_w_out[j])
        x = x + y
        x = x + 0.5 * swiglu_ffn(rms_norm(x, ffn2_norm[i]), ffn2_w_in[i], ffn2_w_out[i])
    return rms_norm(x, final_norm)


_drawn_inputs = setup_inputs


def setup_inputs(seed=0):
    import zlib

    import numpy as np

    out = dict(_drawn_inputs(seed))
    spreads = {}
    factors = {'pool_b': 7.805,
     'conv_b': 3.172,
     'conv_ln_b': 6.462,
     'sgu_ln_g': 3.727,
     'sgu_ln_b': 8.0,
     'sgu_b': 3.485}
    for name, (base, spread) in spreads.items():
        noise = np.random.default_rng([zlib.crc32(name.encode()), seed]).standard_normal(out[name].shape)
        drawn = base * np.exp(spread * noise) if base else spread * noise
        out[name] = __import__('jax').numpy.asarray(drawn.astype(out[name].dtype))
    for name, factor in factors.items():
        out[name] = (out[name] * factor).astype(out[name].dtype)
    return out
```

```python
from contextlib import ExitStack

import concourse.bass as bass
from concourse import mybir

ALU = mybir.AluOpType
ACT = mybir.ActivationFunctionType
F32 = mybir.dt.float32
F32R = mybir.dt.float32r
I32 = mybir.dt.int32

P = 128
EPS = 1e-6
POOL_WINDOWS = (2, 4, 8, 16)

SLAB = 2048
WIDTH = 256
RAW = 3
RING = 6


def at(count, per, i):
    return count if i is None else i * per + count


def hybrid_trunk(nc, x, ffn1_norm, ffn1_w_in, ffn1_w_out, mix_norm, ffn2_norm, ffn2_w_in, ffn2_w_out,
                 ab_w_in, pool_w, pool_b, pool_scale, conv_w, conv_b, conv_ln_g, conv_ln_b, ab_w_out,
                 sgu_w_in, sgu_ln_g, sgu_ln_b, sgu_w, sgu_b, sgu_w_out, final_norm, out):
    _, T, D = x.shape
    TT = T // P
    KD = D // P
    FF = ffn1_w_out.shape[1]
    STEPS = FF // WIDTH
    POOL_CH = pool_scale.shape[1]
    CONV_CH = conv_b.shape[1]
    TAPS = conv_w.shape[1]
    CT = CONV_CH // P
    G = len(POOL_WINDOWS)
    HEADS = sgu_w.shape[1]
    HALF = D // 2
    assert TT == 2 and KD * WIDTH == SLAB and 2 * D == SLAB and STEPS == 11
    assert ffn1_norm.shape[0] == 2 and POOL_CH == G * P and CT == 4 and HEADS == 8 and G == 4

    FFN_SLABS, MIX0_SLABS, MIX1_SLABS = 3 * STEPS, 10, 12
    stages = [("ffn", ffn1_w_in[0], ffn1_w_out[0], ffn1_norm[0]), ("mix0", None, None, mix_norm[0]),
              ("ffn", ffn2_w_in[0], ffn2_w_out[0], ffn2_norm[0]),
              ("ffn", ffn1_w_in[1], ffn1_w_out[1], ffn1_norm[1]), ("mix1", None, None, mix_norm[1]),
              ("ffn", ffn2_w_in[1], ffn2_w_out[1], ffn2_norm[1])]
    gains = [s[3] for s in stages] + [final_norm]
    slabs_of = {"ffn": FFN_SLABS, "mix0": MIX0_SLABS, "mix1": MIX1_SLABS}
    banks_of = {"ffn": STEPS, "mix0": 3, "mix1": 4}
    base, fill0, ffn0 = [0], [0], [0]
    for kind, *_ in stages:
        base.append(base[-1] + slabs_of[kind])
        fill0.append(fill0[-1] + banks_of[kind])
        ffn0.append(ffn0[-1] + (STEPS if kind == "ffn" else 0))
    TOTAL = base[-1]

    order = []
    for k, (kind, *_) in enumerate(stages):
        order += [("norm", k, t, h) for t in range(TT) for h in range(2)]
        if kind == "mix0":
            order += ["taps", "columns", ("pool", 0), ("pool", 1), "mean", "var", "spread"]
        if kind == "mix1":
            order += [("spatial_w", 0), ("spatial_w", 1)] + [("spatial", j) for j in range(4)]
    small = {name: n for n, name in enumerate(order)}

    with ExitStack() as ctx:
        def sb(name, shape, dt=F32):
            return ctx.enter_context(nc.sbuf_tensor(name, shape, dt))

        def sem(name):
            return ctx.enter_context(nc.semaphore(name))

        raw = sb("raw", [P, RAW, SLAB])
        w_hi = sb("w_hi", [P, RING, SLAB], F32R)
        w_lo = sb("w_lo", [P, RING, SLAB], F32R)
        xres = sb("xres", [P, TT, D])
        xs = sb("xs", [P, TT, D])
        xn_hi = sb("xn_hi", [P, KD, T], F32R)
        xn_lo = sb("xn_lo", [P, KD, T], F32R)
        act_hi = sb("act_hi", [P, KD, T], F32R)
        act_lo = sb("act_lo", [P, KD, T], F32R)
        sgh = sb("sgh", [P, 2, 2, T])
        gain = sb("gain", [P, 2, D])
        scratch = sb("scratch", [P, 6144])
        ident = sb("ident", [P, P])
        ones = sb("ones", [P, P])
        avg = sb("avg", [P, P])
        ms = sb("ms", [P, TT, 2])
        ms_eps = sb("ms_eps", [P, TT])
        rstd = sb("rstd", [P, TT])
        minus_half = sb("minus_half", [P, TT])
        cnt_i = sb("cnt_i", [P, 16], I32)
        corr = sb("corr", [P, G, 16])
        taps = sb("taps", [P, CT, TAPS])
        cols = sb("cols", [P, 5, CT])
        stats = sb("stats", [P, TT, 4, 6])
        mv = sb("mv", [P, TT, 2])
        ga = ctx.enter_context(nc.psum_tensor("ga", [P, 2, T], F32))
        ub = ctx.enter_context(nc.psum_tensor("ub", [P, 2, T], F32))
        acc = [[ctx.enter_context(nc.psum_tensor(f"acc{t}{h}", [P, HALF], F32)) for h in range(2)]
               for t in range(TT)]
        tp = [ctx.enter_context(nc.psum_tensor(f"tp{b}", [P, 512], F32)) for b in range(2)]

        PAD = 16
        LEAD = TAPS - 1
        PW = PAD + T
        o = 0
        u_pad = scratch[:, o:o + G * PW].rearrange("p (g t) -> p g t", g=G)
        o += G * PW
        sum_a = scratch[:, o:o + G * PW].rearrange("p (g t) -> p g t", g=G)
        o += G * PW
        sum_b = scratch[:, o:o + G * PW].rearrange("p (g t) -> p g t", g=G)
        o += G * PW
        conv_in = scratch[:, o:o + CT * (LEAD + T)].rearrange("p (c t) -> p c t", c=CT)
        o += CT * (LEAD + T)
        pw = scratch[:, o:o + G * P].rearrange("p (g d) -> p g d", g=G)
        o += G * P
        tap_rows = scratch[0:TAPS, o:o + CONV_CH]
        o += CONV_CH
        col_rows = scratch[0:5 * CT, o:o + P]
        o += P
        diag = scratch[:, o:o + T]
        o += T
        assert o <= 6144
        y = xs[:, 0, :].rearrange("p (c t) -> p c t", c=CT)
        yc = xs[:, 1, :].rearrange("p (c t) -> p c t", c=CT)
        sq = sgh[:, :, :, :].rearrange("p a b t -> p (a b) t")
        uT = scratch[:, 0:KD * T].rearrange("p (k t) -> p k t", k=KD)
        ln_g = scratch[:, 2048:2048 + D]
        ln_b = scratch[:, 3072:3072 + D]
        sb_rep = scratch[:, 4096:4096 + HEADS * P].rearrange("p (h s) -> p h s", h=HEADS)
        spatial_wT = scratch[:, 5120:5120 + HEADS * P].rearrange("p (h s) -> p h s", h=HEADS)
        spatial_w = sgh[:, :, :, :].rearrange("p a b t -> p (a b t)").rearrange("p (h s) -> p h s", h=HEADS)

        x_landed = sem("x_landed")
        gain_landed = [sem(f"gain_landed{i}") for i in range(2)]
        mix0_landed = sem("mix0_landed")
        mix1_landed = sem("mix1_landed")
        spatial_landed = sem("spatial_landed")
        raw_landed = [sem(f"raw_landed{i}") for i in range(RAW)]
        hi_split = sem("hi_split")
        lo_split = sem("lo_split")
        slab_used = sem("slab_used")
        first_out = sem("first_out")
        ga_free = sem("ga_free")
        ub_free = sem("ub_free")
        h_hi_done = sem("h_hi_done")
        h_done = sem("h_done")
        consts = sem("consts")
        corr_done = sem("corr_done")
        x_ready = sem("x_ready")
        ms_ready = sem("ms_ready")
        eps_ready = sem("eps_ready")
        rstd_ready = sem("rstd_ready")
        xs_ready = sem("xs_ready")
        small_full = sem("small_full")
        small_free = sem("small_free")
        xn_hi_ready = sem("xn_hi_ready")
        dve_step = sem("dve_step")
        cols_ready = sem("cols_ready")
        pooled_ready = sem("pooled_ready")
        mixed_ready = sem("mixed_ready")
        mix_hi = sem("mix_hi")
        mix_ready = sem("mix_ready")
        y_ready = sem("y_ready")
        yc_ready = sem("yc_ready")
        sq_ready = sem("sq_ready")
        diag_ready = sem("diag_ready")
        yn_ready = sem("yn_ready")
        post_ready = sem("post_ready")
        mask_ready = sem("mask_ready")
        v_ready = sem("v_ready")
        gu_ready = sem("gu_ready")
        gu_hi = sem("gu_hi")
        gu_done = sem("gu_done")
        out_landed = sem("out_landed")

        block = ctx.enter_context(nc.Block())

        @block.sync
        def _(sp):
            def load(n, src, i=None):
                if n >= RAW or i is not None:
                    sp.wait_ge(lo_split, at(n - RAW + 1, RING, i))
                sp.dma_start(raw[:, n % RAW, :].rearrange("p (c n) -> p c n", n=src.shape[-1]), src)\
                    .then_inc(raw_landed[n % RAW], 16)

            def gain_load(k):
                if k >= 2:
                    sp.wait_ge(xs_ready, 4 * (k - 1))
                sp.dma_start(gain[:, k % 2, :], gains[k].rearrange("(a d) -> a d", a=1).broadcast_to([P, D]))\
                    .then_inc(gain_landed[k % 2], 16)

            def in_view(w):
                return w.rearrange("(c p) n -> p c n", p=P)

            def out_view(w):
                return w.rearrange("(c p) n -> p c n", p=P)

            for t in range(TT):
                sp.dma_start(xres[:, t, :], x[0, t * P:(t + 1) * P, :]).then_inc(x_landed, 16)
                if t == 0:
                    gain_load(0)

            for k, (kind, w_in, w_out, _) in enumerate(stages):
                b = base[k]
                if kind == "ffn":
                    wi, wo = in_view(w_in), out_view(w_out)
                    load(b, wi[:, :, 0:WIDTH])
                    load(b + 1, wi[:, :, FF:FF + WIDTH])
                    if k == 0:
                        sp.dma_start(pw, pool_w[0].rearrange("g c d -> c g d")).then_inc(mix0_landed, 16)
                        sp.wait_ge(consts, 5)
                        sp.dma_start(tap_rows, conv_w[0]).then_inc(mix0_landed, 16)
                        rows = [pool_b[0], pool_scale[0].rearrange("(c p) -> c p", p=P),
                                conv_b[0].rearrange("(c p) -> c p", p=P),
                                conv_ln_g[0].rearrange("(c p) -> c p", p=P),
                                conv_ln_b[0].rearrange("(c p) -> c p", p=P)]
                        for r, src in enumerate(rows):
                            sp.dma_start(col_rows[r * CT:(r + 1) * CT, :], src).then_inc(mix0_landed, 16)
                    def turn(i, run):
                        for j in range(2):
                            n, s = b + 2 + 3 * j, 1 + j
                            load(n, wi[:, :, bass.ds(i * (2 * WIDTH) + s * WIDTH, WIDTH)], run)
                            load(n + 1, wi[:, :, bass.ds(i * (2 * WIDTH) + (FF + s * WIDTH), WIDTH)], run)
                            load(n + 2, wo[:, bass.ds(i * 4 + 2 * (s - 1), 2), :], run)

                    turn(0, None)
                    with sp.Fori(1, (STEPS - 3) // 2) as i:
                        turn(i, i)
                    if k == 2:
                        sp.wait_ge(slab_used, base[2])
                        sp.dma_start(ln_g, sgu_ln_g[0].rearrange("(a d) -> a d", a=1).broadcast_to([P, D]))\
                            .then_inc(mix1_landed, 16)
                        sp.dma_start(ln_b, sgu_ln_b[0].rearrange("(a d) -> a d", a=1).broadcast_to([P, D]))\
                            .then_inc(mix1_landed, 16)
                        sp.dma_start(scratch[:, 4096:4096 + HEADS * P],
                                     sgu_b[0].rearrange("(a h) s -> a (h s)", a=1).broadcast_to([P, HEADS * P]))\
                            .then_inc(mix1_landed, 16)
                    n = b + 2 + 3 * (STEPS - 3)
                    for s in (STEPS - 2, STEPS - 1):
                        load(n, wi[:, :, s * WIDTH:(s + 1) * WIDTH])
                        load(n + 1, wi[:, :, FF + s * WIDTH:FF + (s + 1) * WIDTH])
                        n += 2
                    for s in range(STEPS - 3, STEPS):
                        load(n, wo[:, 2 * s:2 * s + 2, :])
                        n += 1
                elif kind == "mix0":
                    wi, wo = in_view(ab_w_in[0]), out_view(ab_w_out[0])
                    gate, a = POOL_CH + CONV_CH, POOL_CH
                    for j, c in enumerate((gate, a, 0, WIDTH, gate + WIDTH, a + WIDTH)):
                        load(b + j, wi[:, :, c:c + WIDTH])
                    for j in range(4):
                        load(b + 6 + j, wo[:, 2 * j:2 * j + 2, :])
                else:
                    wi, wo = in_view(sgu_w_in[0]), out_view(sgu_w_out[0])
                    for j in range(8):
                        c = (D + j * WIDTH) if j < 4 else (j - 4) * WIDTH
                        load(b + j, wi[:, :, c:c + WIDTH])
                    sp.wait_ge(slab_used, b)
                    sp.dma_start(spatial_w, sgu_w[0].rearrange("h s t -> s h t"))\
                        .then_inc(spatial_landed, 16)
                    for j in range(4):
                        load(b + 8 + j, wo[:, 2 * j:2 * j + 2, :])
                gain_load(k + 1)

            last = len(stages)
            for t in range(TT):
                for h in range(2):
                    sp.wait_ge(xs_ready, 4 * last + 2 * t + h + 1)
                    sp.dma_start(out[0, t * P:(t + 1) * P, h * HALF:(h + 1) * HALF],
                                 xs[:, t, h * HALF:(h + 1) * HALF]).then_inc(out_landed, 16)
            sp.wait_ge(out_landed, 16 * 2 * TT)

        @block.gpsimd
        def _(pool):
            pool.memset(minus_half[:, :], -0.5).then_inc(consts, 1)
            pool.memset(ident[:, :], 0.0).then_inc(consts, 1)
            pool.memset(ones[:, :], 1.0).then_inc(consts, 1)
            pool.memset(avg[:, :], 1.0 / CONV_CH).then_inc(consts, 1)
            pool.memset(scratch[:, 0:3 * G * PW + CT * (LEAD + T)], 0.0).then_inc(consts, 1)
            pool.wait_ge(consts, 5)
            pool.affine_select(out=ident[:, :], in_=ident[:, :], compare_op=ALU.not_equal, fill=1.0,
                               base=0, pattern=[[-1, P]], channel_multiplier=1).then_inc(consts, 1)
            pool.iota(cnt_i[:, :], pattern=[[1, 16]], base=1, channel_multiplier=0).then_inc(consts, 1)

            seen = 0

            def root(lo, hi):
                nonlocal seen
                seen += 1
                pool.wait_ge(eps_ready, seen)
                pool.tensor_tensor(rstd[:, lo:hi], ms_eps[:, lo:hi], minus_half[:, lo:hi], ALU.pow)\
                    .then_inc(rstd_ready, 1)

            for k in range(len(stages) + 1):
                for t in range(TT):
                    root(t, t + 1)
                kind = stages[k][0] if k < len(stages) else None
                if kind == "mix0":
                    root(0, TT)
                if kind == "mix1":
                    pool.wait_ge(spatial_landed, 16)
                    pool.affine_select(out=spatial_w, in_=spatial_w, compare_op=ALU.is_ge, fill=0.0, base=0,
                                       pattern=[[0, HEADS], [-1, P]], channel_multiplier=1)\
                        .then_inc(mask_ready, 1)
                    root(0, TT)

        @block.scalar
        def _(act):
            nxt = 0

            def split(n, i=None):
                act.wait_ge(raw_landed[n % RAW], at(16 * (n // RAW + 1), 16 * RING // RAW, i))
                if n >= RING:
                    act.wait_ge(slab_used, at(n - RING + 1, RING, i))
                act.activation(w_hi[:, n % RING, :], raw[:, n % RAW, :], ACT.Copy).then_inc(hi_split, 1)

            def split_to(n):
                nonlocal nxt
                while nxt <= min(n, TOTAL - 1):
                    split(nxt)
                    nxt += 1

            def norm(k):
                for t in range(TT):
                    for h in range(2):
                        if k == 0:
                            act.wait_ge(x_landed, 16 * TT)
                        else:
                            act.wait_ge(x_ready, 4 * (k - 1) + 2 * t + h + 1)
                        act.activation(xs[:, t, h * HALF:(h + 1) * HALF], xres[:, t, h * HALF:(h + 1) * HALF],
                                       ACT.Square, scale=float(D) ** -0.5,
                                       accum_out=ms[:, t, h:h + 1]).then_inc(ms_ready, 1)
                    if k < len(stages):
                        for h in range(2):
                            n = small[("norm", k, t, h)]
                            act.wait_ge(small_full, n + 1)
                            act.activation(xn_hi[:, 4 * h:4 * h + 4, t * P:(t + 1) * P],
                                           tp[n % 2][:, :].rearrange("p (c t) -> p c t", c=4), ACT.Copy)\
                                .then_inc(xn_hi_ready, 1)

            def gate(n, f, func, i=None, per=2):
                act.wait_ge(slab_used, at(n + 1, RING, i))
                if f:
                    act.wait_ge(ub_free, at(f, per, i))
                act.activation(sgh[:, 0, :, :], ga[:, :, :], func).then_inc(ga_free, 1)

            def product_hi(slot, f, i=None):
                act.wait_ge(ub_free, at(f + 1, 2, i))
                act.activation(act_hi[:, 2 * slot:2 * slot + 2, :], sgh[:, 1, :, :], ACT.Copy)\
                    .then_inc(h_hi_done, 1)

            split_to(RING - 4)
            for k, (kind, *_) in enumerate(stages):
                b, f = base[k], fill0[k]
                norm(k)
                split_to(b + 3)
                if kind == "ffn":
                    gate(b, f, ACT.Silu)
                    split_to(b + 4)
                    product_hi(0, f)
                    split_to(b + 7)
                    with act.Fori(0, (STEPS - 3) // 2) as i:
                        for j in range(2):
                            n, s = b + 2 + 3 * j, 1 + j
                            gate(n, f + s, ACT.Silu, i)
                            split(n + 6, i)
                            product_hi(s % 2, f + s, i)
                            split(n + 7, i)
                            split(n + 8, i)
                    nxt += 3 * (STEPS - 3)
                    n = b + 2 + 3 * (STEPS - 3)
                    for s in (STEPS - 2, STEPS - 1):
                        gate(n, f + s, ACT.Silu)
                        split_to(n + 6)
                        product_hi(1 if s == STEPS - 2 else 2, f + s)
                        split_to(n + 7)
                        n += 2
                elif kind == "mix0":
                    gate(b, f, ACT.Sigmoid)
                    split_to(b + 7)
                    for j, (bank, free) in enumerate(((ga, ga_free), (ub, ub_free))):
                        act.wait_ge(slab_used, b + 3 + j)
                        act.wait_ge(consts, 5)
                        act.activation(u_pad[:, 2 * j:2 * j + 2, PAD:PAD + T], bank[:, :, :], ACT.Copy)\
                            .then_inc(free, 1)
                    split_to(b + 9)
                    gate(b + 4, f + 2, ACT.Sigmoid)
                    for j in range(2):
                        act.wait_ge(mixed_ready, 2 * (j + 1))
                        act.activation(act_hi[:, 2 * j:2 * j + 2, :], sum_a[:, 2 * j:2 * j + 2, PAD:PAD + T],
                                       ACT.Copy).then_inc(mix_hi, 1)
                    split_to(b + 10)
                    act.wait_ge(yc_ready, 1)
                    act.activation(sq, yc, ACT.Square).then_inc(sq_ready, 1)
                    split_to(b + 12)
                    for c in range(CT):
                        act.wait_ge(yn_ready, c // 2 + 1)
                        act.activation(sq[:, c, :], y[:, c, :], ACT.Silu, bias=cols[:, 4, c:c + 1],
                                       scale=cols[:, 3, c:c + 1]).then_inc(post_ready, 1)
                        if c % 2:
                            act.wait_ge(post_ready, c + 1)
                            act.activation(act_hi[:, 3 + c:5 + c, :], sq[:, c - 1:c + 1, :], ACT.Copy)\
                                .then_inc(mix_hi, 1)
                else:
                    for j in range(4):
                        bank, free = ((ga, ga_free), (ub, ub_free))[j % 2]
                        act.wait_ge(slab_used, b + j + 1)
                        act.wait_ge(small_full, small[("norm", k, 1, 1)] + 1)
                        act.activation(xs[:, :, j * WIDTH:(j + 1) * WIDTH], bank[:, :, :], ACT.Gelu)\
                            .then_inc(free, 1)
                        split_to(b + (4, 7, 8, 9)[j])
                    act.wait_ge(mix1_landed, 16 * 3)
                    for j in range(4):
                        bank, free = ((ga, ga_free), (ub, ub_free))[j % 2]
                        act.wait_ge(slab_used, b + 5 + j)
                        act.activation(uT[:, 2 * j:2 * j + 2, :], bank[:, :, :], ACT.Gelu).then_inc(free, 1)
                        split_to(b + 10 + j)
                    for j in range(4):
                        act.wait_ge(gu_ready, j + 1)
                        act.activation(act_hi[:, 2 * j:2 * j + 2, :], uT[:, 2 * j:2 * j + 2, :], ACT.Copy)\
                            .then_inc(gu_hi, 1)
            norm(len(stages))

        @block.vector
        def _(dve):
            nxt = 0
            steps = 0
            roots = 0
            tsplit = []

            def split(n, i=None):
                dve.wait_ge(hi_split, at(n + 1, RING, i))
                dve.tensor_tensor(w_lo[:, n % RING, :], raw[:, n % RAW, :], w_hi[:, n % RING, :].bitcast(F32),
                                  ALU.subtract).then_inc(lo_split, 1)

            def split_to(n):
                nonlocal nxt
                while nxt <= min(n, TOTAL - 1):
                    split(nxt)
                    nxt += 1

            def own(instruction):
                nonlocal steps
                steps += 1
                instruction.then_inc(dve_step, 1)
                return steps

            def root_wait(value):
                nonlocal roots
                roots += 1
                value.then_inc(eps_ready, 1)
                dve.wait_ge(rstd_ready, roots)

            def norm(k):
                for t in range(TT):
                    if k:
                        scale = 0.5 if stages[k - 1][0] == "ffn" else 1.0
                        if t == 0:
                            dve.wait_ge(first_out, k)
                        else:
                            dve.wait_ge(slab_used, base[k])
                        for h in range(2):
                            xh = xres[:, t, h * HALF:(h + 1) * HALF]
                            dve.scalar_tensor_tensor(out=xh, in0=acc[t][h][:, :], scalar=scale, in1=xh,
                                                     op0=ALU.mult, op1=ALU.add).then_inc(x_ready, 1)
                    dve.wait_ge(ms_ready, 4 * k + 2 * t + 2)
                    root_wait(dve.tensor_scalar(ms_eps[:, t:t + 1], ms[:, t, 0:1], ms[:, t, 1:2], EPS,
                                                ALU.add, ALU.add))
                    dve.wait_ge(gain_landed[k % 2], 16 * (k // 2 + 1))
                    for h in range(2):
                        c = slice(h * HALF, (h + 1) * HALF)
                        dve.scalar_tensor_tensor(out=xs[:, t, c], in0=xres[:, t, c], scalar=rstd[:, t:t + 1],
                                                 in1=gain[:, k % 2, c], op0=ALU.mult, op1=ALU.mult)\
                            .then_inc(xs_ready, 1)
                    if k < len(stages):
                        for h in range(2):
                            n = small[("norm", k, t, h)]
                            dve.wait_ge(xn_hi_ready, 4 * k + 2 * t + h + 1)
                            hi = xn_hi[:, 4 * h:4 * h + 4, t * P:(t + 1) * P]
                            dve.tensor_tensor(xn_lo[:, 4 * h:4 * h + 4, t * P:(t + 1) * P],
                                              tp[n % 2][:, :].rearrange("p (c t) -> p c t", c=4),
                                              hi.bitcast(F32), ALU.subtract).then_inc(small_free, 1)

            def product(n, f, e=0, i=None, out=None):
                if e:
                    dve.wait_ge(h_done, at(e, 2, i))
                dve.wait_ge(slab_used, at(n + 1, RING, i))
                dve.wait_ge(ga_free, at(f + 1, 2, i))
                dve.tensor_tensor(sgh[:, 1, :, :] if out is None else out, ub[:, :, :], sgh[:, 0, :, :],
                                  ALU.mult).then_inc(ub_free, 1)

            def product_lo(slot, e, i=None):
                dve.wait_ge(h_hi_done, at(e + 1, 2, i))
                dve.tensor_tensor(act_lo[:, 2 * slot:2 * slot + 2, :], sgh[:, 1, :, :],
                                  act_hi[:, 2 * slot:2 * slot + 2, :].bitcast(F32), ALU.subtract)\
                    .then_inc(h_done, 1)

            dve.wait_ge(consts, 7)
            for g, w in enumerate(POOL_WINDOWS):
                dve.tensor_scalar(corr[:, g, :], cnt_i[:, :], float(w), 1.0 / w, ALU.min, ALU.mult)\
                    .then_inc(corr_done, 1)
            dve.wait_ge(corr_done, G)
            dve.reciprocal(corr[:, :, :], corr[:, :, :]).then_inc(corr_done, 1)

            split_to(RING - 4)
            for k, (kind, *_) in enumerate(stages):
                b, f, e = base[k], fill0[k], ffn0[k]
                norm(k)
                split_to(b + 3)
                if kind == "ffn":
                    split_to(b + 4)
                    product(b + 1, f, e)
                    product_lo(0, e)
                    split_to(b + 7)
                    with dve.Fori(0, (STEPS - 3) // 2) as i:
                        for j in range(2):
                            n, s = b + 2 + 3 * j, 1 + j
                            split(n + 6, i)
                            product(n + 1, f + s, e + s, i)
                            product_lo(s % 2, e + s, i)
                            split(n + 7, i)
                            split(n + 8, i)
                    nxt += 3 * (STEPS - 3)
                    n = b + 2 + 3 * (STEPS - 3)
                    for s in (STEPS - 2, STEPS - 1):
                        split_to(n + 6)
                        product(n + 1, f + s, e + s)
                        product_lo(1 if s == STEPS - 2 else 2, e + s)
                        split_to(n + 7)
                        n += 2
                elif kind == "mix0":
                    dve.wait_ge(consts, 5)
                    product(b + 1, f, out=conv_in[:, 0:2, LEAD:LEAD + T])
                    split_to(b + 7)
                    n = small["taps"]
                    dve.wait_ge(small_full, n + 1)
                    dve.tensor_copy(taps[:, :, :], tp[n % 2][:, 0:CT * TAPS].rearrange("p (c k) -> p c k", c=CT))\
                        .then_inc(small_free, 1)
                    n = small["columns"]
                    dve.wait_ge(small_full, n + 1)
                    dve.tensor_copy(cols[:, :, :], tp[n % 2][:, 0:5 * CT].rearrange("p (r c) -> p r c", c=CT))\
                        .then_inc(small_free, 1)
                    dve.wait_ge(small_free, n + 1)

                    def conv(c0):
                        nonlocal steps
                        first = steps
                        for c in (c0, c0 + 1):
                            own(dve.tensor_scalar(y[:, c, :], conv_in[:, c, 0:T], taps[:, c, 0:1],
                                                  cols[:, 2, c:c + 1], ALU.mult, ALU.add))
                        with dve.Fori(0, (TAPS - 1) // 5) as i:
                            for q in range(1, 6):
                                for a, c in enumerate((c0, c0 + 1)):
                                    dve.wait_ge(dve_step, at(first + 2 * (q - 1) + a + 1, 10, i))
                                    dve.scalar_tensor_tensor(
                                        out=y[:, c, :], in0=conv_in[:, c, bass.ds(i * 5 + q, T)],
                                        scalar=taps[:, c, bass.ds(i * 5 + q, 1)], in1=y[:, c, :],
                                        op0=ALU.mult, op1=ALU.add).then_inc(dve_step, 1)
                        steps = first + 2 * TAPS
                        return steps

                    conv(0)

                    dve.wait_ge(ub_free, f + 2)
                    dve.wait_ge(ga_free, f + 2)
                    src, dst, reach = u_pad, sum_a, 1
                    for g in range(G):
                        s = own(dve.tensor_tensor(dst[:, g:G, PAD:], src[:, g:G, PAD:],
                                                  src[:, g:G, PAD - reach:PW - reach], ALU.add))
                        dve.wait_ge(dve_step, s)
                        src, dst, reach = dst, (sum_b if g % 2 == 0 else sum_a), 2 * reach
                    dve.wait_ge(corr_done, G + 1)
                    for g in range(G):
                        sums = (sum_a, sum_b)[g % 2]
                        s = own(dve.tensor_tensor(sums[:, g, PAD:PAD + 16], sums[:, g, PAD:PAD + 16],
                                                  corr[:, g, :], ALU.mult))
                    dve.wait_ge(dve_step, s)
                    for g, w in enumerate(POOL_WINDOWS):
                        sums = (sum_a, sum_b)[g % 2]
                        dve.scalar_tensor_tensor(out=u_pad[:, g, PAD:], in0=sums[:, g, PAD:], scalar=1.0 / w,
                                                 in1=u_pad[:, g, PAD:], op0=ALU.mult, op1=ALU.subtract)\
                            .then_inc(pooled_ready, 1)
                    product(b + 5, f + 2, out=conv_in[:, 2:4, LEAD:LEAD + T])
                    for j in range(2):
                        n = small[("pool", j)]
                        dve.wait_ge(small_full, n + 1)
                        for a in range(2):
                            g = 2 * j + a
                            dve.tensor_scalar(sum_a[:, g, PAD:], tp[n % 2][:, a * T:(a + 1) * T],
                                              cols[:, 0, g:g + 1], cols[:, 1, g:g + 1], ALU.add, ALU.mult)\
                                .then_inc(mixed_ready, 1)
                    for j in range(2):
                        dve.wait_ge(mix_hi, j + 1)
                        dve.tensor_tensor(act_lo[:, 2 * j:2 * j + 2, :], sum_a[:, 2 * j:2 * j + 2, PAD:],
                                          act_hi[:, 2 * j:2 * j + 2, :].bitcast(F32), ALU.subtract)\
                            .then_inc(mix_ready, 1)
                        dve.wait_ge(mix_ready, j + 1)
                        dve.engine_nop().then_inc(small_free, 1)
                    split_to(b + 9)
                    dve.wait_ge(dve_step, conv(2))
                    dve.engine_nop().then_inc(y_ready, 1)
                    n = small["mean"]
                    dve.wait_ge(small_full, n + 1)
                    mean = tp[n % 2][:, 0:T].rearrange("p (a t) -> p a t", a=1).broadcast_to([P, CT, T])
                    dve.tensor_tensor(yc, y, mean, ALU.subtract).then_inc(yc_ready, 1)
                    dve.wait_ge(yc_ready, 1)
                    dve.engine_nop().then_inc(small_free, 1)
                    split_to(b + 10)
                    n = small["var"]
                    dve.wait_ge(small_full, n + 1)
                    own(dve.tensor_scalar(ms_eps[:, :], tp[n % 2][:, 0:TT], EPS, None, ALU.add))
                    dve.wait_ge(dve_step, steps)
                    dve.engine_nop().then_inc(small_free, 1)
                    root_wait(dve.engine_nop())
                    for t in range(TT):
                        dve.tensor_scalar(diag[:, t * P:(t + 1) * P], ident[:, :], rstd[:, t:t + 1], None,
                                          ALU.mult).then_inc(diag_ready, 1)
                    n = small["spread"]
                    dve.wait_ge(small_full, n + 1)
                    spread = tp[n % 2][:, 0:T].rearrange("p (a t) -> p a t", a=1).broadcast_to([P, 2, T])
                    for j in range(2):
                        dve.tensor_tensor(y[:, 2 * j:2 * j + 2, :], yc[:, 2 * j:2 * j + 2, :], spread, ALU.mult)\
                            .then_inc(yn_ready, 1)
                    dve.wait_ge(yn_ready, 2)
                    dve.engine_nop().then_inc(small_free, 1)
                    for j in range(2):
                        dve.wait_ge(mix_hi, j + 3)
                        dve.tensor_tensor(act_lo[:, 4 + 2 * j:6 + 2 * j, :], sq[:, 2 * j:2 * j + 2, :],
                                          act_hi[:, 4 + 2 * j:6 + 2 * j, :].bitcast(F32), ALU.subtract)\
                            .then_inc(mix_ready, 1)
                    split_to(b + 12)
                else:
                    for j in range(4):
                        free = (ga_free, ub_free)[j % 2]
                        dve.wait_ge(free, f + j // 2 + 1)
                        for t in range(TT):
                            s = own(dve.bn_stats(stats[:, t, j, :], xs[:, t, j * WIDTH:(j + 1) * WIDTH]))
                        split_to(b + (4, 7, 8, 8)[j])
                    dve.wait_ge(dve_step, s)
                    for t in range(TT):
                        s = own(dve.bn_aggr(mv[:, t, :], stats[:, t, :, :].rearrange("p a b -> p (a b)")))
                    dve.wait_ge(dve_step, s)
                    root_wait(dve.tensor_scalar(ms_eps[:, :], mv[:, :, 1], EPS, None, ALU.add))
                    dve.wait_ge(mix1_landed, 16 * 3)
                    for t in range(TT):
                        s = own(dve.scalar_tensor_tensor(out=xs[:, t, :], in0=xs[:, t, :], scalar=mv[:, t, 0:1],
                                                         in1=ln_g, op0=ALU.subtract, op1=ALU.mult))
                    for t in range(TT):
                        dve.wait_ge(dve_step, s - 1 + t)
                        dve.scalar_tensor_tensor(out=xs[:, t, :], in0=xs[:, t, :], scalar=rstd[:, t:t + 1],
                                                 in1=ln_b, op0=ALU.mult, op1=ALU.add).then_inc(v_ready, 1)
                    for j in range(2):
                        n = small[("spatial_w", j)]
                        dve.wait_ge(small_full, n + 1)
                        dve.tensor_copy(spatial_wT[:, 4 * j:4 * j + 4, :],
                                        tp[n % 2][:, :].rearrange("p (h s) -> p h s", h=4)).then_inc(small_free, 1)
                    split_to(b + 11)
                    for j in range(4):
                        if j == 2:
                            split_to(b + 13)
                        n = small[("spatial", j)]
                        dve.wait_ge(small_full, n + 1)
                        tmp = sgh[:, j % 2, :, :]
                        bias = sb_rep[:, 2 * j:2 * j + 2, :].rearrange("p h (a s) -> p h a s", a=1)\
                            .broadcast_to([P, 2, TT, P])
                        dve.tensor_tensor(tmp.rearrange("p h (a s) -> p h a s", a=TT),
                                          tp[n % 2][:, :].rearrange("p (h a s) -> p h a s", h=2, a=TT),
                                          bias, ALU.add).then_inc(small_free, 1)
                        dve.wait_ge(small_free, n + 1)
                        dve.wait_ge((ga_free, ub_free)[j % 2], f + 2 + j // 2 + 1)
                        dve.tensor_tensor(uT[:, 2 * j:2 * j + 2, :], tmp, uT[:, 2 * j:2 * j + 2, :], ALU.mult)\
                            .then_inc(gu_ready, 1)
                        dve.wait_ge(gu_hi, j + 1)
                        dve.tensor_tensor(act_lo[:, 2 * j:2 * j + 2, :], uT[:, 2 * j:2 * j + 2, :],
                                          act_hi[:, 2 * j:2 * j + 2, :].bitcast(F32), ALU.subtract)\
                            .then_inc(gu_done, 1)
            norm(len(stages))

        @block.tensor
        def _(pe):
            def three(dst, s_hi, s_lo, m_hi, m_lo, start, stop):
                pe.matmul(dst, s_hi, m_hi, start=start, stop=False)
                pe.matmul(dst, s_hi, m_lo, start=False, stop=False)
                return pe.matmul(dst, s_lo, m_hi, start=False, stop=stop)

            def slab_ready(n, i=None):
                pe.wait_ge(lo_split, at(n + 1, RING, i))

            def ring(w, n, c, a, m):
                return w[:, n % RING, c * (SLAB // m) + a:c * (SLAB // m) + a + P] if m == KD else None

            def slab_in(n, bank, tokens, halves=None):
                for j in range(2):
                    for c in range(KD):
                        if halves is not None and j == 0 and c % 4 == 0:
                            pe.wait_ge(small_free, halves + c // 4 + 1)
                        o = c * WIDTH + j * P
                        mm = three(bank[:, j, tokens], w_hi[:, n % RING, o:o + P], w_lo[:, n % RING, o:o + P],
                                   xn_hi[:, c, tokens], xn_lo[:, c, tokens], c == 0, c == KD - 1)
                return mm

            def slab_in_rows(n, bank, t, halves=None):
                tok = slice(t * P, (t + 1) * P)
                for c in range(KD):
                    if halves is not None and c % 4 == 0:
                        pe.wait_ge(small_free, halves + c // 4 + 1)
                    o = slice(c * WIDTH, (c + 1) * WIDTH)
                    mm = three(bank[:, t, :], xn_hi[:, c, tok], xn_lo[:, c, tok], w_hi[:, n % RING, o],
                               w_lo[:, n % RING, o], c == 0, c == KD - 1)
                return mm

            def slab_out(n, t, tile, start, stop):
                tok = slice(t * P, (t + 1) * P)
                for c in range(2):
                    for h in range(2):
                        o = slice(c * D + h * HALF, c * D + (h + 1) * HALF)
                        mm = three(acc[t][h][:, :], act_hi[:, tile + c, tok], act_lo[:, tile + c, tok],
                                   w_hi[:, n % RING, o], w_lo[:, n % RING, o], start and c == 0, stop and c == 1)
                return mm

            def small_bank(name):
                n = small[name]
                if n >= 2:
                    pe.wait_ge(small_free, n - 1)
                return tp[n % 2]

            def transposes(k, t):
                for h in range(2):
                    bank = small_bank(("norm", k, t, h))
                    pe.wait_ge(xs_ready, 4 * k + 2 * t + h + 1)
                    for c in range(4):
                        o = h * HALF + c * P
                        mm = pe.transpose(bank[:, c * P:(c + 1) * P], xs[:, t, o:o + P], ident[:, :])
                    mm.then_inc(small_full, 1)

            def first_pair(k, do, f):
                b = base[k]
                for t in range(TT):
                    transposes(k, t)
                    for a, (bank, free) in enumerate(((ga, ga_free), (ub, ub_free))):
                        if t == 0:
                            if f:
                                pe.wait_ge(free, f)
                            slab_ready(b + a)
                        mm = do(b + a, bank, t, small[("norm", k, t, 0)] if a == 0 else None)
                        if t == TT - 1:
                            mm.then_inc(slab_used, 1)

            def in_cols(n, bank, t, halves):
                return slab_in(n, bank, slice(t * P, (t + 1) * P), halves)

            def full_in(n, which, f, i=None, per=2):
                bank, free = ((ga, ga_free), (ub, ub_free))[which]
                slab_ready(n, i)
                pe.wait_ge(free, at(f, per, i))
                slab_in(n, bank, slice(0, T)).then_inc(slab_used, 1)

            def tail(slabs, ready):
                for t in range(TT):
                    for a, (n, tile) in enumerate(slabs):
                        if t == 0:
                            slab_ready(n)
                            ready(a)
                        mm = slab_out(n, t, tile, first_slab == n, a == len(slabs) - 1)
                        if t == TT - 1:
                            mm.then_inc(slab_used, 1)
                    if t == 0:
                        mm.then_inc(first_out, 1)

            pe.wait_ge(consts, 6)
            for k, (kind, *_) in enumerate(stages):
                b, f, e = base[k], fill0[k], ffn0[k]
                if kind == "ffn":
                    first_pair(k, in_cols, f)

                    def step_out(n, slot, done, start, i=None):
                        slab_ready(n, i)
                        pe.wait_ge(h_done, at(done, 2, i))
                        for t in range(TT):
                            mm = slab_out(n, t, 2 * slot, start, False)
                        mm.then_inc(slab_used, 1)

                    full_in(b + 2, 0, f + 1)
                    full_in(b + 3, 1, f + 1)
                    step_out(b + 4, 0, e + 1, True)
                    full_in(b + 5, 0, f + 2)
                    full_in(b + 6, 1, f + 2)
                    step_out(b + 7, 1, e + 2, False)
                    with pe.Fori(1, (STEPS - 3) // 2) as i:
                        for j in range(2):
                            n, s = b + 2 + 3 * j, 1 + j
                            full_in(n, 0, f + s, i)
                            full_in(n + 1, 1, f + s, i)
                            step_out(n + 2, (s - 1) % 2, e + s, False, i)
                    n = b + 2 + 3 * (STEPS - 3)
                    for s in (STEPS - 2, STEPS - 1):
                        full_in(n, 0, f + s)
                        full_in(n + 1, 1, f + s)
                        n += 2
                    first_slab = None
                    tail([(n + a, 2 * a) for a in range(3)],
                         lambda a: pe.wait_ge(h_done, e + STEPS - 2 + a))
                elif kind == "mix0":
                    first_pair(k, in_cols, f)
                    pe.wait_ge(mix0_landed, 16 * 7)
                    bank = small_bank("taps")
                    for c in range(CT):
                        mm = pe.transpose(bank[:, c * TAPS:(c + 1) * TAPS], tap_rows[:, c * P:(c + 1) * P],
                                          ident[0:TAPS, 0:TAPS])
                    mm.then_inc(small_full, 1)
                    pe.transpose(small_bank("columns")[:, 0:5 * CT], col_rows, ident[0:5 * CT, 0:5 * CT])\
                        .then_inc(small_full, 1)
                    for j in range(4):
                        full_in(b + 2 + j, j % 2, f + 1 + j // 2)
                    for j in range(2):
                        bank = small_bank(("pool", j))
                        for a in range(2):
                            g = 2 * j + a
                            pe.wait_ge(pooled_ready, g + 1)
                            mm = pe.matmul(bank[:, a * T:(a + 1) * T], pw[:, g, :], u_pad[:, g, PAD:],
                                           start=True, stop=True)
                        mm.then_inc(small_full, 1)
                    for j in range(2):
                        slab_ready(b + 6 + j)
                        pe.wait_ge(mix_ready, j + 1)
                        for t in range(TT):
                            mm = slab_out(b + 6 + j, t, 2 * j, j == 0, False)
                        mm.then_inc(slab_used, 1)
                    bank = small_bank("mean")
                    pe.wait_ge(y_ready, 1)
                    for c in range(CT):
                        mm = pe.matmul(bank[:, 0:T], avg[:, :], y[:, c, :], start=c == 0, stop=c == CT - 1)
                    mm.then_inc(small_full, 1)
                    bank = small_bank("var")
                    pe.wait_ge(sq_ready, 1)
                    for t in range(TT):
                        for c in range(CT):
                            mm = pe.matmul(bank[:, t:t + 1], sq[:, c, t * P:(t + 1) * P], avg[:, 0:1],
                                           start=c == 0, stop=c == CT - 1)
                    mm.then_inc(small_full, 1)
                    bank = small_bank("spread")
                    pe.wait_ge(diag_ready, TT)
                    pe.matmul(bank[:, 0:T], ones[:, :], diag, start=True, stop=True).then_inc(small_full, 1)
                    first_slab = None
                    tail([(b + 8, 4), (b + 9, 6)], lambda a: pe.wait_ge(mix_ready, 3 + a))
                else:
                    first_pair(k, slab_in_rows, f)
                    for j in range(2, 4):
                        bank, free = ((ga, ga_free), (ub, ub_free))[j % 2]
                        slab_ready(b + j)
                        pe.wait_ge(free, f + 1)
                        for t in range(TT):
                            mm = slab_in_rows(b + j, bank, t)
                        mm.then_inc(slab_used, 1)
                    full_in(b + 4, 0, f + 2)
                    full_in(b + 5, 1, f + 2)
                    for j in range(2):
                        bank = small_bank(("spatial_w", j))
                        pe.wait_ge(mask_ready, 1)
                        for a in range(4):
                            mm = pe.transpose(bank[:, a * P:(a + 1) * P], spatial_w[:, 4 * j + a, :], ident[:, :])
                        mm.then_inc(small_full, 1)
                    full_in(b + 6, 0, f + 3)

                    def spatial(j):
                        bank = small_bank(("spatial", j))
                        pe.wait_ge(small_free, small[("spatial_w", 1)] + 1)
                        for a in range(2):
                            for t in range(TT):
                                h = 2 * j + a
                                pe.wait_ge(v_ready, t + 1)
                                o = (a * TT + t) * P
                                mm = pe.matmul(bank[:, o:o + P], xs[:, t, h * P:(h + 1) * P], spatial_wT[:, h, :],
                                               start=True, stop=True)
                        mm.then_inc(small_full, 1)

                    spatial(0)
                    spatial(1)
                    full_in(b + 7, 1, f + 3)
                    spatial(2)
                    spatial(3)
                    first_slab = b + 8
                    tail([(b + 8 + j, 2 * j) for j in range(4)], lambda a: pe.wait_ge(gu_done, a + 1))


_INS = ['x', 'ffn1_norm', 'ffn1_w_in', 'ffn1_w_out', 'mix_norm', 'ffn2_norm', 'ffn2_w_in', 'ffn2_w_out',
        'ab_w_in', 'pool_w', 'pool_b', 'pool_scale', 'conv_w', 'conv_b', 'conv_ln_g', 'conv_ln_b', 'ab_w_out',
        'sgu_w_in', 'sgu_ln_g', 'sgu_ln_b', 'sgu_w', 'sgu_b', 'sgu_w_out', 'final_norm']
_OUTS = [((1, 256, 1024), 'float32')]


def kernel(**inputs):
    import numpy as _np
    import concourse.bacc as _bacc
    from concourse import mybir as _mybir
    from concourse.bass_utils import run_bass_kernel_spmd as _run

    nc = _bacc.Bacc("TRN2", target_bir_lowering=False, num_devices=1)
    arrays, args = {}, []
    for name in _INS:
        a = _np.ascontiguousarray(inputs[name])
        arrays[f"in_{name}_dram"] = a
        args.append(nc.dram_tensor(f"in_{name}_dram", a.shape, _mybir.dt.from_np(a.dtype), kind="ExternalInput").ap())
    for i, (shape, dtype) in enumerate(_OUTS):
        dt = _mybir.dt.from_np(_np.dtype(dtype))
        args.append(nc.dram_tensor(f"out_{i}_dram", shape, dt, kind="ExternalOutput").ap())
    hybrid_trunk(nc, *args)
    r = _run(nc, [arrays], core_ids=[0])
    got = tuple(r.results[0][f"out_{i}_dram"] for i in range(len(_OUTS)))
    return got[0]
```

```python
from contextlib import ExitStack

import concourse.bass as bass
from concourse import mybir

ALU = mybir.AluOpType
ACT = mybir.ActivationFunctionType
F32 = mybir.dt.float32
F32R = mybir.dt.float32r
I32 = mybir.dt.int32

P = 128
EPS = 1e-6
POOL_WINDOWS = (2, 4, 8, 16)

SLAB = 2048
WIDTH = 256
RAW = 3
RING = 6


def at(count, per, i):
    return count if i is None else i * per + count


def hybrid_trunk(nc, x, ffn1_norm, ffn1_w_in, ffn1_w_out, mix_norm, ffn2_norm, ffn2_w_in, ffn2_w_out,
                 ab_w_in, pool_w, pool_b, pool_scale, conv_w, conv_b, conv_ln_g, conv_ln_b, ab_w_out,
                 sgu_w_in, sgu_ln_g, sgu_ln_b, sgu_w, sgu_b, sgu_w_out, final_norm, out):
    _, T, D = x.shape
    TT = T // P
    KD = D // P
    FF = ffn1_w_out.shape[1]
    STEPS = FF // WIDTH
    POOL_CH = pool_scale.shape[1]
    CONV_CH = conv_b.shape[1]
    TAPS = conv_w.shape[1]
    CT = CONV_CH // P
    G = len(POOL_WINDOWS)
    HEADS = sgu_w.shape[1]
    HALF = D // 2
    assert TT == 2 and KD * WIDTH == SLAB and 2 * D == SLAB and STEPS == 11
    assert ffn1_norm.shape[0] == 2 and POOL_CH == G * P and CT == 4 and HEADS == 8 and G == 4

    FFN_SLABS, MIX0_SLABS, MIX1_SLABS = 3 * STEPS, 10, 12
    stages = [("ffn", ffn1_w_in[0], ffn1_w_out[0], ffn1_norm[0]), ("mix0", None, None, mix_norm[0]),
              ("ffn", ffn2_w_in[0], ffn2_w_out[0], ffn2_norm[0]),
              ("ffn", ffn1_w_in[1], ffn1_w_out[1], ffn1_norm[1]), ("mix1", None, None, mix_norm[1]),
              ("ffn", ffn2_w_in[1], ffn2_w_out[1], ffn2_norm[1])]
    gains = [s[3] for s in stages] + [final_norm]
    slabs_of = {"ffn": FFN_SLABS, "mix0": MIX0_SLABS, "mix1": MIX1_SLABS}
    banks_of = {"ffn": STEPS, "mix0": 3, "mix1": 4}
    base, fill0, ffn0 = [0], [0], [0]
    for kind, *_ in stages:
        base.append(base[-1] + slabs_of[kind])
        fill0.append(fill0[-1] + banks_of[kind])
        ffn0.append(ffn0[-1] + (STEPS if kind == "ffn" else 0))
    TOTAL = base[-1]

    order = []
    for k, (kind, *_) in enumerate(stages):
        order += [("norm", k, t, h) for t in range(TT) for h in range(2)]
        if kind != "mix1":
            order += [("hidden", k)]
        if k == 0:
            order += ["taps", "columns"]
        if kind == "mix0":
            order += [("pooled", 0), ("pooled", 1), ("pool", 0), ("pool", 1), "mean", "var", "spread"]
        if kind == "mix1":
            order += [("spatial_w", 0), ("spatial_w", 1)] + [("spatial", j) for j in range(4)]
    small = {name: n for n, name in enumerate(order)}

    with ExitStack() as ctx:
        def sb(name, shape, dt=F32):
            return ctx.enter_context(nc.sbuf_tensor(name, shape, dt))

        def sem(name):
            return ctx.enter_context(nc.semaphore(name))

        raw = sb("raw", [P, RAW, SLAB])
        w_hi = sb("w_hi", [P, RING, SLAB], F32R)
        w_lo = sb("w_lo", [P, RING, SLAB], F32R)
        xres = sb("xres", [P, TT, D])
        xs = sb("xs", [P, TT, D])
        xn_hi = sb("xn_hi", [P, KD, T], F32R)
        xn_lo = sb("xn_lo", [P, KD, T], F32R)
        act_hi = sb("act_hi", [P, KD, T], F32R)
        act_lo = sb("act_lo", [P, KD, T], F32R)
        sgh = sb("sgh", [P, 2, 2, T])
        gain = sb("gain", [P, 2, D])
        scratch = sb("scratch", [P, 6144])
        ident = sb("ident", [P, P])
        ones = sb("ones", [P, P])
        avg = sb("avg", [P, P])
        ms = sb("ms", [P, TT, 2])
        ms_eps = sb("ms_eps", [P, TT])
        rstd = sb("rstd", [P, TT])
        minus_half = sb("minus_half", [P, TT])
        cnt_i = sb("cnt_i", [P, 16], I32)
        share = sb("share", [P, G, 16])
        pool_bias = sb("pool_bias", [P, G])
        warm = sb("warm", [P, 1])
        taps = sb("taps", [P, CT, TAPS])
        cols = sb("cols", [P, 5, CT])
        stats = sb("stats", [P, TT, 4, 6])
        mv = sb("mv", [P, TT, 2])
        CONSTS = 11
        ga = ctx.enter_context(nc.psum_tensor("ga", [P, 2, T], F32))
        ub = ctx.enter_context(nc.psum_tensor("ub", [P, 2, T], F32))
        acc = [[ctx.enter_context(nc.psum_tensor(f"acc{t}{h}", [P, HALF], F32)) for h in range(2)]
               for t in range(TT)]
        tp = [ctx.enter_context(nc.psum_tensor(f"tp{b}", [P, 512], F32)) for b in range(2)]

        LEAD = TAPS - 1
        o = 0

        def space(n, rows=P):
            nonlocal o
            o += n
            assert o <= scratch.shape[1]
            return scratch[0:rows, o - n:o]

        u = space(TT * POOL_CH).rearrange("p (t c) -> p t c", t=TT)
        mixed = u.rearrange("p t c -> p (t c)").rearrange("p (g t) -> p g t", g=G)
        pooled = space(G * T).rearrange("p (g t) -> p g t", g=G)
        conv_in = space(CT * (LEAD + T)).rearrange("p (c t) -> p c t", c=CT)
        pw = space(G * P).rearrange("p (g d) -> p g d", g=G)
        tap_rows = space(CONV_CH, TAPS)
        col_rows = space(P, 5 * CT)
        window = space(G * 3 * P).rearrange("p (g b t) -> p g b t", g=G, b=3)
        diag = space(T)
        y = xs[:, 0, :].rearrange("p (c t) -> p c t", c=CT)
        yc = xs[:, 1, :].rearrange("p (c t) -> p c t", c=CT)
        sq = sgh[:, :, :, :].rearrange("p a b t -> p (a b) t")
        uT = scratch[:, 0:KD * T].rearrange("p (k t) -> p k t", k=KD)
        ln_g = scratch[:, 2048:2048 + D]
        ln_b = scratch[:, 3072:3072 + D]
        sb_rep = scratch[:, 4096:4096 + HEADS * P].rearrange("p (h s) -> p h s", h=HEADS)
        spatial_wT = scratch[:, 5120:5120 + HEADS * P].rearrange("p (h s) -> p h s", h=HEADS)
        spatial_w = sgh[:, :, :, :].rearrange("p a b t -> p (a b t)").rearrange("p (h s) -> p h s", h=HEADS)

        x_landed = [sem(f"x_landed{t}") for t in range(TT)]
        gain_landed = [sem(f"gain_landed{i}") for i in range(2)]
        mix0_landed = sem("mix0_landed")
        mix1_landed = sem("mix1_landed")
        spatial_landed = sem("spatial_landed")
        raw_landed = [sem(f"raw_landed{i}") for i in range(RAW)]
        hi_split = sem("hi_split")
        lo_split = sem("lo_split")
        slab_used = sem("slab_used")
        first_out = sem("first_out")
        ga_free = sem("ga_free")
        ub_free = sem("ub_free")
        h_hi_done = sem("h_hi_done")
        h_done = sem("h_done")
        consts = sem("consts")
        share_done = sem("share_done")
        pool_step = sem("pool_step")
        window_done = sem("window_done")
        x_ready = sem("x_ready")
        ms_ready = sem("ms_ready")
        eps_ready = sem("eps_ready")
        rstd_ready = sem("rstd_ready")
        xs_ready = sem("xs_ready")
        small_full = sem("small_full")
        small_free = sem("small_free")
        xn_hi_ready = sem("xn_hi_ready")
        dve_step = sem("dve_step")
        conv_step = sem("conv_step")
        cols_ready = sem("cols_ready")
        mixed_ready = sem("mixed_ready")
        mix_hi = sem("mix_hi")
        mix_ready = sem("mix_ready")
        sq_ready = sem("sq_ready")
        diag_ready = sem("diag_ready")
        yn_ready = sem("yn_ready")
        post_ready = sem("post_ready")
        mask_ready = sem("mask_ready")
        v_ready = sem("v_ready")
        gu_ready = sem("gu_ready")
        gu_hi = sem("gu_hi")
        gu_done = sem("gu_done")
        out_landed = sem("out_landed")

        block = ctx.enter_context(nc.Block())

        @block.sync
        def _(sp):
            def load(n, src, i=None):
                if n >= RAW or i is not None:
                    sp.wait_ge(lo_split, at(n - RAW + 1, RING, i))
                sp.dma_start(raw[:, n % RAW, :].rearrange("p (c n) -> p c n", n=src.shape[-1]), src)\
                    .then_inc(raw_landed[n % RAW], 16)

            def gain_load(k):
                if k >= 2:
                    sp.wait_ge(xs_ready, 4 * (k - 1))
                sp.dma_start(gain[:, k % 2, :], gains[k].rearrange("(a d) -> a d", a=1).broadcast_to([P, D]))\
                    .then_inc(gain_landed[k % 2], 16)

            def in_view(w):
                return w.rearrange("(c p) n -> p c n", p=P)

            def out_view(w):
                return w.rearrange("(c p) n -> p c n", p=P)

            sp.dma_start(xres[:, 0, :], x[0, 0:P, :]).then_inc(x_landed[0], 16)

            for k, (kind, w_in, w_out, _) in enumerate(stages):
                b = base[k]
                if kind == "ffn":
                    wi, wo = in_view(w_in), out_view(w_out)
                    load(b, wi[:, :, 0:WIDTH])
                    if k == 0:
                        gain_load(0)
                        for t in range(1, TT):
                            sp.dma_start(xres[:, t, :], x[0, t * P:(t + 1) * P, :]).then_inc(x_landed[t], 16)
                    load(b + 1, wi[:, :, FF:FF + WIDTH])
                    def turn(i, run):
                        for j in range(2):
                            n, s = b + 2 + 3 * j, 1 + j
                            load(n, wi[:, :, bass.ds(i * (2 * WIDTH) + s * WIDTH, WIDTH)], run)
                            load(n + 1, wi[:, :, bass.ds(i * (2 * WIDTH) + (FF + s * WIDTH), WIDTH)], run)
                            load(n + 2, wo[:, bass.ds(i * 4 + 2 * (s - 1), 2), :], run)

                    turn(0, None)
                    if k == 0:
                        sp.dma_start(pw, pool_w[0].rearrange("g c d -> c g d")).then_inc(mix0_landed, 16)
                        sp.dma_start(tap_rows, conv_w[0]).then_inc(mix0_landed, 16)
                        rows = [pool_b[0], pool_scale[0].rearrange("(c p) -> c p", p=P),
                                conv_b[0].rearrange("(c p) -> c p", p=P),
                                conv_ln_g[0].rearrange("(c p) -> c p", p=P),
                                conv_ln_b[0].rearrange("(c p) -> c p", p=P)]
                        for r, src in enumerate(rows):
                            sp.dma_start(col_rows[r * CT:(r + 1) * CT, :], src).then_inc(mix0_landed, 16)
                    with sp.Fori(1, (STEPS - 3) // 2) as i:
                        turn(i, i)
                    if k == 2:
                        sp.wait_ge(slab_used, base[2])
                        sp.dma_start(ln_g, sgu_ln_g[0].rearrange("(a d) -> a d", a=1).broadcast_to([P, D]))\
                            .then_inc(mix1_landed, 16)
                        sp.dma_start(ln_b, sgu_ln_b[0].rearrange("(a d) -> a d", a=1).broadcast_to([P, D]))\
                            .then_inc(mix1_landed, 16)
                        sp.dma_start(scratch[:, 4096:4096 + HEADS * P],
                                     sgu_b[0].rearrange("(a h) s -> a (h s)", a=1).broadcast_to([P, HEADS * P]))\
                            .then_inc(mix1_landed, 16)
                    n = b + 2 + 3 * (STEPS - 3)
                    for s in (STEPS - 2, STEPS - 1):
                        load(n, wi[:, :, s * WIDTH:(s + 1) * WIDTH])
                        load(n + 1, wi[:, :, FF + s * WIDTH:FF + (s + 1) * WIDTH])
                        n += 2
                    for s in range(STEPS - 3, STEPS):
                        load(n, wo[:, 2 * s:2 * s + 2, :])
                        n += 1
                elif kind == "mix0":
                    wi, wo = in_view(ab_w_in[0]), out_view(ab_w_out[0])
                    gate, a = POOL_CH + CONV_CH, POOL_CH
                    for j, c in enumerate((gate, a, 0, WIDTH, gate + WIDTH, a + WIDTH)):
                        load(b + j, wi[:, :, c:c + WIDTH])
                    for j in range(4):
                        load(b + 6 + j, wo[:, 2 * j:2 * j + 2, :])
                else:
                    wi, wo = in_view(sgu_w_in[0]), out_view(sgu_w_out[0])
                    for j in range(8):
                        c = (D + j * WIDTH) if j < 4 else (j - 4) * WIDTH
                        load(b + j, wi[:, :, c:c + WIDTH])
                    sp.wait_ge(slab_used, b)
                    sp.dma_start(spatial_w, sgu_w[0].rearrange("h s t -> s h t"))\
                        .then_inc(spatial_landed, 16)
                    for j in range(4):
                        load(b + 8 + j, wo[:, 2 * j:2 * j + 2, :])
                gain_load(k + 1)

            last = len(stages)
            for t in range(TT):
                for h in range(2):
                    sp.wait_ge(xs_ready, 4 * last + 2 * t + h + 1)
                    sp.dma_start(out[0, t * P:(t + 1) * P, h * HALF:(h + 1) * HALF],
                                 xs[:, t, h * HALF:(h + 1) * HALF]).then_inc(out_landed, 16)
            sp.wait_ge(out_landed, 16 * 2 * TT)

        @block.gpsimd
        def _(pool):
            pool.memset(minus_half[:, :], -0.5).then_inc(consts, 1)
            pool.memset(ident[:, :], 0.0).then_inc(consts, 1)
            pool.memset(ones[:, :], 1.0).then_inc(consts, 1)
            pool.memset(avg[:, :], 1.0 / CONV_CH).then_inc(consts, 1)
            for g, w in enumerate(POOL_WINDOWS):
                pool.memset(window[:, g, :, :], 1.0 / w).then_inc(consts, 1)
            pool.memset(conv_in[:, :, 0:LEAD], 0.0).then_inc(consts, 1)
            pool.iota(cnt_i[:, :], pattern=[[1, 16]], base=1, channel_multiplier=0).then_inc(consts, 1)
            pool.wait_ge(consts, CONSTS - 1)
            pool.affine_select(out=ident[:, :], in_=ident[:, :], compare_op=ALU.not_equal, fill=1.0,
                               base=0, pattern=[[-1, P]], channel_multiplier=1).then_inc(consts, 1)

            def windows():
                pool.wait_ge(share_done, G + 2)
                n = 0
                for lo, hi in ((0, 2), (2, 3)):
                    part = window[:, :, lo:hi, :].rearrange("p g b t -> p g (b t)")
                    pool.affine_select(out=part, in_=part, compare_op=ALU.is_ge, fill=0.0, base=0,
                                       pattern=[[0, G], [1, (hi - lo) * P]], channel_multiplier=-1)\
                        .then_inc(pool_step, 1)
                    n += 1
                pool.wait_ge(pool_step, n)
                for lo, hi in ((0, 2), (2, 3)):
                    for g, w in enumerate(POOL_WINDOWS):
                        part = window[:, g, lo:hi, :].rearrange("p b t -> p (b t)")
                        pool.affine_select(out=part, in_=part, compare_op=ALU.is_ge, fill=0.0, base=w - 1,
                                           pattern=[[-1, (hi - lo) * P]], channel_multiplier=1)\
                            .then_inc(pool_step, 1)
                        n += 1
                pool.wait_ge(pool_step, n)
                pool.wait_ge(consts, CONSTS)
                same = ident[:, :].rearrange("p (g t) -> p g t", g=1).broadcast_to([P, G, P])
                for block in (0, 2):
                    pool.tensor_tensor(window[:, :, block, :], window[:, :, block, :], same, ALU.subtract)\
                        .then_inc(window_done, 1)

            seen = 0

            def root(lo, hi):
                nonlocal seen
                seen += 1
                pool.wait_ge(eps_ready, seen)
                pool.tensor_tensor(rstd[:, lo:hi], ms_eps[:, lo:hi], minus_half[:, lo:hi], ALU.pow)\
                    .then_inc(rstd_ready, 1)

            for k in range(len(stages) + 1):
                for t in range(TT):
                    root(t, t + 1)
                if k == 0:
                    windows()
                kind = stages[k][0] if k < len(stages) else None
                if kind == "mix0":
                    root(0, TT)
                if kind == "mix1":
                    pool.wait_ge(spatial_landed, 16)
                    pool.affine_select(out=spatial_w, in_=spatial_w, compare_op=ALU.is_ge, fill=0.0, base=0,
                                       pattern=[[0, HEADS], [-1, P]], channel_multiplier=1)\
                        .then_inc(mask_ready, 1)
                    root(0, TT)

        @block.scalar
        def _(act):
            nxt = 0

            def split(n, i=None):
                act.wait_ge(raw_landed[n % RAW], at(16 * (n // RAW + 1), 16 * RING // RAW, i))
                if n >= RING:
                    act.wait_ge(slab_used, at(n - RING + 1, RING, i))
                act.activation(w_hi[:, n % RING, :], raw[:, n % RAW, :], ACT.Copy).then_inc(hi_split, 1)

            def split_to(n):
                nonlocal nxt
                while nxt <= min(n, TOTAL - 1):
                    split(nxt)
                    nxt += 1

            def norm(k, t):
                for h in range(2):
                    if k == 0:
                        act.wait_ge(x_landed[t], 16)
                    else:
                        act.wait_ge(x_ready, 4 * (k - 1) + 2 * t + h + 1)
                    act.activation(xs[:, t, h * HALF:(h + 1) * HALF], xres[:, t, h * HALF:(h + 1) * HALF],
                                   ACT.Square, scale=float(D) ** -0.5,
                                   accum_out=ms[:, t, h:h + 1]).then_inc(ms_ready, 1)
                if k < len(stages):
                    for h in range(2):
                        n = small[("norm", k, t, h)]
                        act.wait_ge(small_full, n + 1)
                        act.activation(xn_hi[:, 4 * h:4 * h + 4, t * P:(t + 1) * P],
                                       tp[n % 2][:, :].rearrange("p (c t) -> p c t", c=4), ACT.Copy)\
                            .then_inc(xn_hi_ready, 1)

            def gate(n, f, func, i=None, per=2):
                act.wait_ge(slab_used, at(n + 1, RING, i))
                if f:
                    act.wait_ge(ub_free, at(f, per, i))
                act.activation(sgh[:, 0, :, :], ga[:, :, :], func).then_inc(ga_free, 1)

            def product_hi(slot, f, i=None):
                act.wait_ge(ub_free, at(f + 1, 2, i))
                act.activation(act_hi[:, 2 * slot:2 * slot + 2, :], sgh[:, 1, :, :], ACT.Copy)\
                    .then_inc(h_hi_done, 1)

            for k, (kind, *_) in enumerate(stages):
                b, f = base[k], fill0[k]
                norm(k, 0)
                split_to(b)
                norm(k, 1)
                split_to(b + 3)
                if kind == "ffn":
                    gate(b, f, ACT.Silu)
                    split_to(b + 5)
                    n = small[("hidden", k)]
                    act.wait_ge(small_full, n + 1)
                    act.activation(act_hi[:, 0:2, :], tp[n % 2][:, :].rearrange("p (j t) -> p j t", j=2), ACT.Copy)\
                        .then_inc(h_hi_done, 1)
                    split_to(b + 7)
                    with act.Fori(0, (STEPS - 3) // 2) as i:
                        for j in range(2):
                            n, s = b + 2 + 3 * j, 1 + j
                            gate(n, f + s, ACT.Silu, i)
                            split(n + 6, i)
                            product_hi(s % 2, f + s, i)
                            split(n + 7, i)
                            split(n + 8, i)
                    nxt += 3 * (STEPS - 3)
                    n = b + 2 + 3 * (STEPS - 3)
                    for s in (STEPS - 2, STEPS - 1):
                        gate(n, f + s, ACT.Silu)
                        split_to(n + 6)
                        product_hi(1 if s == STEPS - 2 else 2, f + s)
                        split_to(n + 7)
                        n += 2
                elif kind == "mix0":
                    gate(b, f, ACT.Sigmoid)
                    split_to(b + 4)
                    n = small[("hidden", k)]
                    act.wait_ge(small_full, n + 1)
                    act.wait_ge(consts, CONSTS)
                    act.activation(conv_in[:, 0:2, LEAD:], tp[n % 2][:, :].rearrange("p (j t) -> p j t", j=2),
                                   ACT.Copy).then_inc(small_free, 1)
                    for j, (bank, free) in enumerate(((ga, ga_free), (ub, ub_free))):
                        act.wait_ge(slab_used, b + 3 + j)
                        act.activation(u[:, :, j * WIDTH:(j + 1) * WIDTH], bank[:, :, :], ACT.Copy)\
                            .then_inc(free, 1)
                        split_to(b + (5, 7)[j])
                    gate(b + 4, f + 2, ACT.Sigmoid)
                    act.activation(warm[:, :], ident[:, 0:1], ACT.Silu)
                    for j in range(2):
                        n = small[("pooled", j)]
                        act.wait_ge(small_full, n + 1)
                        act.activation(pooled[:, 2 * j:2 * j + 2, :],
                                       tp[n % 2][:, :].rearrange("p (g t) -> p g t", g=2), ACT.Copy)\
                            .then_inc(small_free, 1)
                    act.wait_ge(cols_ready, 1)
                    for j in range(2):
                        n = small[("pool", j)]
                        act.wait_ge(small_full, n + 1)
                        for a, done in ((0, mixed_ready), (1, small_free)):
                            g = 2 * j + a
                            act.activation(mixed[:, g, :], tp[n % 2][:, a * T:(a + 1) * T], ACT.Identity,
                                           bias=pool_bias[:, g:g + 1], scale=cols[:, 1, g:g + 1]).then_inc(done, 1)
                        act.wait_ge(mixed_ready, j + 1)
                        act.wait_ge(small_free, n + 1)
                        act.activation(act_hi[:, 2 * j:2 * j + 2, :], mixed[:, 2 * j:2 * j + 2, :], ACT.Copy)\
                            .then_inc(mix_hi, 1)
                    split_to(b + 9)
                    act.wait_ge(small_free, small["mean"] + 1)
                    act.activation(sq, yc, ACT.Square).then_inc(sq_ready, 1)
                    split_to(b + 10)
                    for c in range(CT):
                        if c < 2:
                            act.wait_ge(yn_ready, 1)
                        else:
                            act.wait_ge(small_free, small["spread"] + 1)
                        act.activation(sq[:, c, :], y[:, c, :], ACT.Silu, bias=cols[:, 4, c:c + 1],
                                       scale=cols[:, 3, c:c + 1]).then_inc(post_ready, 1)
                        if c % 2:
                            act.wait_ge(post_ready, c + 1)
                            act.activation(act_hi[:, 3 + c:5 + c, :], sq[:, c - 1:c + 1, :], ACT.Copy)\
                                .then_inc(mix_hi, 1)
                    split_to(b + 12)
                else:
                    for j in range(4):
                        bank, free = ((ga, ga_free), (ub, ub_free))[j % 2]
                        act.wait_ge(slab_used, b + j + 1)
                        act.wait_ge(small_full, small[("norm", k, 1, 1)] + 1)
                        act.activation(xs[:, :, j * WIDTH:(j + 1) * WIDTH], bank[:, :, :], ACT.Gelu)\
                            .then_inc(free, 1)
                        split_to(b + (4, 7, 8, 9)[j])
                    act.wait_ge(mix1_landed, 16 * 3)
                    for j in range(4):
                        bank, free = ((ga, ga_free), (ub, ub_free))[j % 2]
                        act.wait_ge(slab_used, b + 5 + j)
                        act.activation(uT[:, 2 * j:2 * j + 2, :], bank[:, :, :], ACT.Gelu).then_inc(free, 1)
                        split_to(b + 10 + j)
                    for j in range(4):
                        act.wait_ge(gu_ready, j + 1)
                        act.activation(act_hi[:, 2 * j:2 * j + 2, :], uT[:, 2 * j:2 * j + 2, :], ACT.Copy)\
                            .then_inc(gu_hi, 1)
            for t in range(TT):
                norm(len(stages), t)

        @block.vector
        def _(dve):
            nxt = 0
            steps = 0
            roots = 0
            tsplit = []

            def split(n, i=None):
                dve.wait_ge(hi_split, at(n + 1, RING, i))
                dve.tensor_tensor(w_lo[:, n % RING, :], raw[:, n % RAW, :], w_hi[:, n % RING, :].bitcast(F32),
                                  ALU.subtract).then_inc(lo_split, 1)

            def split_to(n):
                nonlocal nxt
                while nxt <= min(n, TOTAL - 1):
                    split(nxt)
                    nxt += 1

            def own(instruction):
                nonlocal steps
                steps += 1
                instruction.then_inc(dve_step, 1)
                return steps

            def root_wait(value):
                nonlocal roots
                roots += 1
                value.then_inc(eps_ready, 1)
                dve.wait_ge(rstd_ready, roots)

            def norm(k, t):
                if k:
                    scale = 0.5 if stages[k - 1][0] == "ffn" else 1.0
                    if t == 0:
                        dve.wait_ge(first_out, k)
                    else:
                        dve.wait_ge(slab_used, base[k])
                    for h in range(2):
                        xh = xres[:, t, h * HALF:(h + 1) * HALF]
                        dve.scalar_tensor_tensor(out=xh, in0=acc[t][h][:, :], scalar=scale, in1=xh,
                                                 op0=ALU.mult, op1=ALU.add).then_inc(x_ready, 1)
                dve.wait_ge(ms_ready, 4 * k + 2 * t + 2)
                root_wait(dve.tensor_scalar(ms_eps[:, t:t + 1], ms[:, t, 0:1], ms[:, t, 1:2], EPS,
                                            ALU.add, ALU.add))
                dve.wait_ge(gain_landed[k % 2], 16 * (k // 2 + 1))
                for h in range(2):
                    c = slice(h * HALF, (h + 1) * HALF)
                    dve.scalar_tensor_tensor(out=xs[:, t, c], in0=xres[:, t, c], scalar=rstd[:, t:t + 1],
                                             in1=gain[:, k % 2, c], op0=ALU.mult, op1=ALU.mult)\
                        .then_inc(xs_ready, 1)
                if k < len(stages):
                    for h in range(2):
                        n = small[("norm", k, t, h)]
                        dve.wait_ge(xn_hi_ready, 4 * k + 2 * t + h + 1)
                        hi = xn_hi[:, 4 * h:4 * h + 4, t * P:(t + 1) * P]
                        dve.tensor_tensor(xn_lo[:, 4 * h:4 * h + 4, t * P:(t + 1) * P],
                                          tp[n % 2][:, :].rearrange("p (c t) -> p c t", c=4),
                                          hi.bitcast(F32), ALU.subtract).then_inc(small_free, 1)

            def product(n, f, e=0, i=None, out=None):
                if e:
                    dve.wait_ge(h_done, at(e, 2, i))
                dve.wait_ge(slab_used, at(n + 1, RING, i))
                dve.wait_ge(ga_free, at(f + 1, 2, i))
                dve.tensor_tensor(sgh[:, 1, :, :] if out is None else out, ub[:, :, :], sgh[:, 0, :, :],
                                  ALU.mult).then_inc(ub_free, 1)

            def product_lo(slot, e, i=None):
                dve.wait_ge(h_hi_done, at(e + 1, 2, i))
                dve.tensor_tensor(act_lo[:, 2 * slot:2 * slot + 2, :], sgh[:, 1, :, :],
                                  act_hi[:, 2 * slot:2 * slot + 2, :].bitcast(F32), ALU.subtract)\
                    .then_inc(h_done, 1)

            def shares():
                dve.wait_ge(consts, CONSTS - 1)
                for g, w in enumerate(POOL_WINDOWS):
                    dve.tensor_scalar(share[:, g, :], cnt_i[:, :], float(w), None, ALU.min)\
                        .then_inc(share_done, 1)
                dve.wait_ge(share_done, G)
                dve.reciprocal(share[:, :, :], share[:, :, :]).then_inc(share_done, 1)
                dve.wait_ge(share_done, G + 1)
                dve.tensor_copy(window[:, :, 0, 0:16], share[:, :, :]).then_inc(share_done, 1)

            for k, (kind, *_) in enumerate(stages):
                b, f, e = base[k], fill0[k], ffn0[k]
                norm(k, 0)
                split_to(b)
                norm(k, 1)
                split_to(b + 3)
                if k == 0:
                    shares()
                if kind == "ffn":
                    split_to(b + 4)
                    product(b + 1, f, e)
                    split_to(b + 5)
                    n = small[("hidden", k)]
                    dve.wait_ge(h_hi_done, e + 1)
                    dve.tensor_tensor(act_lo[:, 0:2, :], tp[n % 2][:, :].rearrange("p (j t) -> p j t", j=2),
                                      act_hi[:, 0:2, :].bitcast(F32), ALU.subtract).then_inc(h_done, 1)
                    dve.wait_ge(h_done, e + 1)
                    dve.engine_nop().then_inc(small_free, 1)
                    split_to(b + 7)
                    with dve.Fori(0, (STEPS - 3) // 2) as i:
                        for j in range(2):
                            n, s = b + 2 + 3 * j, 1 + j
                            split(n + 6, i)
                            product(n + 1, f + s, e + s, i)
                            product_lo(s % 2, e + s, i)
                            split(n + 7, i)
                            split(n + 8, i)
                    nxt += 3 * (STEPS - 3)
                    n = b + 2 + 3 * (STEPS - 3)
                    for s in (STEPS - 2, STEPS - 1):
                        split_to(n + 6)
                        product(n + 1, f + s, e + s)
                        product_lo(1 if s == STEPS - 2 else 2, e + s)
                        split_to(n + 7)
                        n += 2
                    if k == 0:
                        n = small["taps"]
                        dve.wait_ge(small_full, n + 1)
                        dve.tensor_copy(taps[:, :, :],
                                        tp[n % 2][:, 0:CT * TAPS].rearrange("p (c k) -> p c k", c=CT))\
                            .then_inc(small_free, 1)
                        n = small["columns"]
                        dve.wait_ge(small_full, n + 1)
                        dve.tensor_copy(cols[:, :, :], tp[n % 2][:, 0:5 * CT].rearrange("p (r c) -> p r c", c=CT))\
                            .then_inc(small_free, 1)
                        dve.wait_ge(small_free, n + 1)
                        dve.tensor_tensor(pool_bias[:, :], cols[:, 0, :], cols[:, 1, :], ALU.mult)\
                            .then_inc(cols_ready, 1)
                elif kind == "mix0":
                    product(b + 1, f, e)
                    split_to(b + 5)
                    turns = (TAPS - 1) // 5

                    def conv(c0, first, last):
                        before = c0 * TAPS
                        if first == 0:
                            for c in (c0, c0 + 1):
                                dve.tensor_scalar(y[:, c, :], conv_in[:, c, 0:T], taps[:, c, 0:1],
                                                  cols[:, 2, c:c + 1], ALU.mult, ALU.add).then_inc(conv_step, 1)
                        with dve.Fori(first, last) as i:
                            for q in range(1, 6):
                                for a, c in enumerate((c0, c0 + 1)):
                                    dve.wait_ge(conv_step, at(before + 2 * (q - 1) + a + 1, 10, i))
                                    dve.scalar_tensor_tensor(
                                        out=y[:, c, :], in0=conv_in[:, c, bass.ds(i * 5 + q, T)],
                                        scalar=taps[:, c, bass.ds(i * 5 + q, 1)], in1=y[:, c, :],
                                        op0=ALU.mult, op1=ALU.add).then_inc(conv_step, 1)

                    dve.wait_ge(small_free, small[("hidden", k)] + 1)
                    conv(0, 0, turns)
                    product(b + 5, f + 2, out=conv_in[:, 2:4, LEAD:])
                    split_to(b + 7)
                    dve.wait_ge(ub_free, f + 3)
                    conv(2, 0, turns // 2)
                    for j in range(2):
                        dve.wait_ge(mix_hi, j + 1)
                        dve.tensor_tensor(act_lo[:, 2 * j:2 * j + 2, :], mixed[:, 2 * j:2 * j + 2, :],
                                          act_hi[:, 2 * j:2 * j + 2, :].bitcast(F32), ALU.subtract)\
                            .then_inc(mix_ready, 1)
                    conv(2, turns // 2, turns)
                    n = small["mean"]
                    dve.wait_ge(small_full, n + 1)
                    mean = tp[n % 2][:, 0:T].rearrange("p (a t) -> p a t", a=1).broadcast_to([P, CT, T])
                    dve.tensor_tensor(yc, y, mean, ALU.subtract).then_inc(small_free, 1)
                    split_to(b + 8)
                    n = small["var"]
                    dve.wait_ge(small_full, n + 1)
                    dve.tensor_scalar(ms_eps[:, :], tp[n % 2][:, 0:TT], EPS, None, ALU.add)\
                        .then_inc(small_free, 1)
                    dve.wait_ge(small_free, n + 1)
                    root_wait(dve.engine_nop())
                    for t in range(TT):
                        dve.tensor_scalar(diag[:, t * P:(t + 1) * P], ident[:, :], rstd[:, t:t + 1], None,
                                          ALU.mult).then_inc(diag_ready, 1)
                    n = small["spread"]
                    dve.wait_ge(small_full, n + 1)
                    spread = tp[n % 2][:, 0:T].rearrange("p (a t) -> p a t", a=1).broadcast_to([P, 2, T])
                    for j, done in enumerate((yn_ready, small_free)):
                        dve.tensor_tensor(y[:, 2 * j:2 * j + 2, :], yc[:, 2 * j:2 * j + 2, :], spread, ALU.mult)\
                            .then_inc(done, 1)
                    split_to(b + 9)
                    for j in range(2):
                        dve.wait_ge(mix_hi, j + 3)
                        dve.tensor_tensor(act_lo[:, 4 + 2 * j:6 + 2 * j, :], sq[:, 2 * j:2 * j + 2, :],
                                          act_hi[:, 4 + 2 * j:6 + 2 * j, :].bitcast(F32), ALU.subtract)\
                            .then_inc(mix_ready, 1)
                    split_to(b + 12)
                else:
                    for j in range(4):
                        free = (ga_free, ub_free)[j % 2]
                        dve.wait_ge(free, f + j // 2 + 1)
                        for t in range(TT):
                            s = own(dve.bn_stats(stats[:, t, j, :], xs[:, t, j * WIDTH:(j + 1) * WIDTH]))
                        split_to(b + (4, 7, 8, 8)[j])
                    dve.wait_ge(dve_step, s)
                    for t in range(TT):
                        s = own(dve.bn_aggr(mv[:, t, :], stats[:, t, :, :].rearrange("p a b -> p (a b)")))
                    dve.wait_ge(dve_step, s)
                    root_wait(dve.tensor_scalar(ms_eps[:, :], mv[:, :, 1], EPS, None, ALU.add))
                    dve.wait_ge(mix1_landed, 16 * 3)
                    for t in range(TT):
                        s = own(dve.scalar_tensor_tensor(out=xs[:, t, :], in0=xs[:, t, :], scalar=mv[:, t, 0:1],
                                                         in1=ln_g, op0=ALU.subtract, op1=ALU.mult))
                    for t in range(TT):
                        dve.wait_ge(dve_step, s - 1 + t)
                        dve.scalar_tensor_tensor(out=xs[:, t, :], in0=xs[:, t, :], scalar=rstd[:, t:t + 1],
                                                 in1=ln_b, op0=ALU.mult, op1=ALU.add).then_inc(v_ready, 1)
                    for j in range(2):
                        n = small[("spatial_w", j)]
                        dve.wait_ge(small_full, n + 1)
                        dve.tensor_copy(spatial_wT[:, 4 * j:4 * j + 4, :],
                                        tp[n % 2][:, :].rearrange("p (h s) -> p h s", h=4)).then_inc(small_free, 1)
                    split_to(b + 11)
                    for j in range(4):
                        if j == 2:
                            split_to(b + 13)
                        n = small[("spatial", j)]
                        dve.wait_ge(small_full, n + 1)
                        tmp = sgh[:, j % 2, :, :]
                        bias = sb_rep[:, 2 * j:2 * j + 2, :].rearrange("p h (a s) -> p h a s", a=1)\
                            .broadcast_to([P, 2, TT, P])
                        dve.tensor_tensor(tmp.rearrange("p h (a s) -> p h a s", a=TT),
                                          tp[n % 2][:, :].rearrange("p (h a s) -> p h a s", h=2, a=TT),
                                          bias, ALU.add).then_inc(small_free, 1)
                        dve.wait_ge(small_free, n + 1)
                        dve.wait_ge((ga_free, ub_free)[j % 2], f + 2 + j // 2 + 1)
                        dve.tensor_tensor(uT[:, 2 * j:2 * j + 2, :], tmp, uT[:, 2 * j:2 * j + 2, :], ALU.mult)\
                            .then_inc(gu_ready, 1)
                        dve.wait_ge(gu_hi, j + 1)
                        dve.tensor_tensor(act_lo[:, 2 * j:2 * j + 2, :], uT[:, 2 * j:2 * j + 2, :],
                                          act_hi[:, 2 * j:2 * j + 2, :].bitcast(F32), ALU.subtract)\
                            .then_inc(gu_done, 1)
            for t in range(TT):
                norm(len(stages), t)

        @block.tensor
        def _(pe):
            def three(dst, s_hi, s_lo, m_hi, m_lo, start, stop):
                pe.matmul(dst, s_hi, m_hi, start=start, stop=False)
                pe.matmul(dst, s_hi, m_lo, start=False, stop=False)
                return pe.matmul(dst, s_lo, m_hi, start=False, stop=stop)

            def slab_ready(n, i=None):
                pe.wait_ge(lo_split, at(n + 1, RING, i))

            def slab_in(n, bank):
                for j in range(2):
                    for c in range(KD):
                        o = c * WIDTH + j * P
                        mm = three(bank[:, j, :], w_hi[:, n % RING, o:o + P], w_lo[:, n % RING, o:o + P],
                                   xn_hi[:, c, :], xn_lo[:, c, :], c == 0, c == KD - 1)
                return mm

            def slab_in_rows(n, bank, t, fresh=None, between=None):
                tok = slice(t * P, (t + 1) * P)
                for c in range(KD):
                    if fresh is not None and c % 4 == 0:
                        pe.wait_ge(small_free, fresh + c // 4 + 1)
                    if between is not None and c == KD - 2:
                        between()
                    o = slice(c * WIDTH, (c + 1) * WIDTH)
                    mm = three(bank[:, t, :], xn_hi[:, c, tok], xn_lo[:, c, tok], w_hi[:, n % RING, o],
                               w_lo[:, n % RING, o], c == 0, c == KD - 1)
                return mm

            def slab_out(n, t, tile, start, stop, between=None):
                tok = slice(t * P, (t + 1) * P)
                for c in range(2):
                    if between is not None and c == 1:
                        between()
                    for h in range(2):
                        o = slice(c * D + h * HALF, c * D + (h + 1) * HALF)
                        mm = three(acc[t][h][:, :], act_hi[:, tile + c, tok], act_lo[:, tile + c, tok],
                                   w_hi[:, n % RING, o], w_lo[:, n % RING, o], start and c == 0, stop and c == 1)
                return mm

            def small_bank(name):
                n = small[name]
                if n >= 2:
                    pe.wait_ge(small_free, n - 1)
                return tp[n % 2]

            def transposes(k, t):
                for h in range(2):
                    bank = small_bank(("norm", k, t, h))
                    pe.wait_ge(xs_ready, 4 * k + 2 * t + h + 1)
                    for c in range(4):
                        o = h * HALF + c * P
                        mm = pe.transpose(bank[:, c * P:(c + 1) * P], xs[:, t, o:o + P], ident[:, :])
                    mm.then_inc(small_full, 1)

            def first_pair(k, f):
                b = base[k]
                pairs = [(t, a) for t in range(TT) for a in range(2)]
                if k == 0:
                    pairs.sort(key=lambda p: p[1])
                for t, a in pairs:
                    bank, free = ((ga, ga_free), (ub, ub_free))[a]
                    if t == 0:
                        if f:
                            pe.wait_ge(free, f)
                        slab_ready(b + a)
                    here = (0, 0 if k == 0 else 1)
                    mm = slab_in_rows(b + a, bank, t, small[("norm", k, t, 0)] if a == 0 else None,
                                      (lambda: transposes(k, 1)) if (t, a) == here else None)
                    if t == TT - 1:
                        mm.then_inc(slab_used, 1)

            def hidden(k, f):
                bank = small_bank(("hidden", k))
                pe.wait_ge(ub_free, f + 1)
                for j in range(2):
                    for t in range(TT):
                        o = j * T + t * P
                        mm = pe.transpose(bank[:, o:o + P], sgh[:, 1, t, j * P:(j + 1) * P], ident[:, :])
                mm.then_inc(small_full, 1)

            def open_bank(n, which, f, i=None, per=2):
                bank, free = ((ga, ga_free), (ub, ub_free))[which]
                slab_ready(n, i)
                pe.wait_ge(free, at(f, per, i))
                return bank

            def full_in(n, which, f, i=None, per=2):
                slab_in(n, open_bank(n, which, f, i, per)).then_inc(slab_used, 1)

            def tail(k, slabs, ready, start=None):
                for t in range(TT):
                    for a, (n, tile) in enumerate(slabs):
                        last = a == len(slabs) - 1
                        if t == 0:
                            slab_ready(n)
                            ready(a)
                        between = None
                        if last and t == TT - 1 and k + 1 < len(stages):
                            between = lambda: transposes(k + 1, 0)
                        mm = slab_out(n, t, tile, start == n, last, between)
                        if t == TT - 1:
                            mm.then_inc(slab_used, 1)
                    if t == 0:
                        mm.then_inc(first_out, 1)

            pe.wait_ge(consts, CONSTS)
            transposes(0, 0)
            for k, (kind, *_) in enumerate(stages):
                b, f, e = base[k], fill0[k], ffn0[k]
                if kind == "ffn":
                    first_pair(k, f)

                    def step_out(n, slot, done, start, i=None):
                        slab_ready(n, i)
                        pe.wait_ge(h_done, at(done, 2, i))
                        for t in range(TT):
                            mm = slab_out(n, t, 2 * slot, start, False)
                        mm.then_inc(slab_used, 1)

                    full_in(b + 2, 0, f + 1)
                    hidden(k, f)
                    full_in(b + 3, 1, f + 1)
                    step_out(b + 4, 0, e + 1, True)
                    full_in(b + 5, 0, f + 2)
                    full_in(b + 6, 1, f + 2)
                    step_out(b + 7, 1, e + 2, False)
                    with pe.Fori(1, (STEPS - 3) // 2) as i:
                        for j in range(2):
                            n, s = b + 2 + 3 * j, 1 + j
                            full_in(n, 0, f + s, i)
                            full_in(n + 1, 1, f + s, i)
                            step_out(n + 2, (s - 1) % 2, e + s, False, i)
                    n = b + 2 + 3 * (STEPS - 3)
                    for s in (STEPS - 2, STEPS - 1):
                        full_in(n, 0, f + s)
                        full_in(n + 1, 1, f + s)
                        n += 2
                    if k == 0:
                        pe.wait_ge(mix0_landed, 16 * 7)
                        bank = small_bank("taps")
                        for c in range(CT):
                            mm = pe.transpose(bank[:, c * TAPS:(c + 1) * TAPS], tap_rows[:, c * P:(c + 1) * P],
                                              ident[0:TAPS, 0:TAPS])
                        mm.then_inc(small_full, 1)
                        pe.transpose(small_bank("columns")[:, 0:5 * CT], col_rows, ident[0:5 * CT, 0:5 * CT])\
                            .then_inc(small_full, 1)
                    tail(k, [(n + a, 2 * a) for a in range(3)],
                         lambda a: pe.wait_ge(h_done, e + STEPS - 2 + a))
                elif kind == "mix0":
                    first_pair(k, f)
                    bank = open_bank(b + 2, 0, f + 1)
                    slab_in_rows(b + 2, bank, 0)
                    hidden(k, f)
                    slab_in_rows(b + 2, bank, 1).then_inc(slab_used, 1)
                    bank = open_bank(b + 3, 1, f + 1)
                    slab_in_rows(b + 3, bank, 0)
                    slab_in_rows(b + 3, bank, 1).then_inc(slab_used, 1)
                    full_in(b + 4, 0, f + 2)
                    full_in(b + 5, 1, f + 2)
                    pe.wait_ge(window_done, 2)
                    pe.wait_ge(ga_free, f + 2)
                    pe.wait_ge(ub_free, f + 2)
                    for j in range(2):
                        bank = small_bank(("pooled", j))
                        for a in range(2):
                            g = 2 * j + a
                            pe.matmul(bank[:, a * T:(a + 1) * T], u[:, 0, g * P:(g + 1) * P],
                                      window[:, g, 0:2, :].rearrange("p b t -> p (b t)"), start=True, stop=False)
                            mm = pe.matmul(bank[:, a * T + P:(a + 1) * T], u[:, 1, g * P:(g + 1) * P],
                                           window[:, g, 2, :], start=False, stop=True)
                        mm.then_inc(small_full, 1)
                    for j in range(2):
                        bank = small_bank(("pool", j))
                        pe.wait_ge(small_free, small[("pooled", j)] + 1)
                        for a in range(2):
                            g = 2 * j + a
                            mm = pe.matmul(bank[:, a * T:(a + 1) * T], pw[:, g, :], pooled[:, g, :],
                                           start=True, stop=True)
                        mm.then_inc(small_full, 1)
                    mean = small_bank("mean")

                    def mean_of(c0):
                        pe.wait_ge(conv_step, (c0 + 2) * TAPS)
                        for c in (c0, c0 + 1):
                            mm = pe.matmul(mean[:, 0:T], avg[:, :], y[:, c, :], start=c == 0, stop=c == CT - 1)
                        return mm

                    mean_of(0)
                    for j in range(2):
                        slab_ready(b + 6 + j)
                        pe.wait_ge(mix_ready, j + 1)
                        for t in range(TT):
                            mm = slab_out(b + 6 + j, t, 2 * j, j == 0, False)
                        mm.then_inc(slab_used, 1)
                    mean_of(2).then_inc(small_full, 1)
                    bank = small_bank("var")
                    pe.wait_ge(sq_ready, 1)
                    for t in range(TT):
                        for c in range(CT):
                            mm = pe.matmul(bank[:, t:t + 1], sq[:, c, t * P:(t + 1) * P], avg[:, 0:1],
                                           start=c == 0, stop=c == CT - 1)
                    mm.then_inc(small_full, 1)
                    bank = small_bank("spread")
                    pe.wait_ge(diag_ready, TT)
                    pe.matmul(bank[:, 0:T], ones[:, :], diag, start=True, stop=True).then_inc(small_full, 1)
                    tail(k, [(b + 8, 4), (b + 9, 6)], lambda a: pe.wait_ge(mix_ready, 3 + a))
                else:
                    first_pair(k, f)
                    for j in range(2, 4):
                        bank, free = ((ga, ga_free), (ub, ub_free))[j % 2]
                        slab_ready(b + j)
                        pe.wait_ge(free, f + 1)
                        for t in range(TT):
                            mm = slab_in_rows(b + j, bank, t)
                        mm.then_inc(slab_used, 1)
                    full_in(b + 4, 0, f + 2)
                    full_in(b + 5, 1, f + 2)
                    for j in range(2):
                        bank = small_bank(("spatial_w", j))
                        pe.wait_ge(mask_ready, 1)
                        for a in range(4):
                            mm = pe.transpose(bank[:, a * P:(a + 1) * P], spatial_w[:, 4 * j + a, :], ident[:, :])
                        mm.then_inc(small_full, 1)
                    full_in(b + 6, 0, f + 3)

                    def spatial(j):
                        bank = small_bank(("spatial", j))
                        pe.wait_ge(small_free, small[("spatial_w", 1)] + 1)
                        for a in range(2):
                            for t in range(TT):
                                h = 2 * j + a
                                pe.wait_ge(v_ready, t + 1)
                                o = (a * TT + t) * P
                                mm = pe.matmul(bank[:, o:o + P], xs[:, t, h * P:(h + 1) * P], spatial_wT[:, h, :],
                                               start=True, stop=True)
                        mm.then_inc(small_full, 1)

                    spatial(0)
                    spatial(1)
                    full_in(b + 7, 1, f + 3)
                    spatial(2)
                    spatial(3)
                    tail(k, [(b + 8 + j, 2 * j) for j in range(4)], lambda a: pe.wait_ge(gu_done, a + 1), b + 8)


_INS = ['x', 'ffn1_norm', 'ffn1_w_in', 'ffn1_w_out', 'mix_norm', 'ffn2_norm', 'ffn2_w_in', 'ffn2_w_out',
        'ab_w_in', 'pool_w', 'pool_b', 'pool_scale', 'conv_w', 'conv_b', 'conv_ln_g', 'conv_ln_b', 'ab_w_out',
        'sgu_w_in', 'sgu_ln_g', 'sgu_ln_b', 'sgu_w', 'sgu_b', 'sgu_w_out', 'final_norm']
_OUTS = [((1, 256, 1024), 'float32')]


def kernel(**inputs):
    import numpy as _np
    import concourse.bacc as _bacc
    from concourse import mybir as _mybir
    from concourse.bass_utils import run_bass_kernel_spmd as _run

    nc = _bacc.Bacc("TRN2", target_bir_lowering=False, num_devices=1)
    arrays, args = {}, []
    for name in _INS:
        a = _np.ascontiguousarray(inputs[name])
        arrays[f"in_{name}_dram"] = a
        args.append(nc.dram_tensor(f"in_{name}_dram", a.shape, _mybir.dt.from_np(a.dtype), kind="ExternalInput").ap())
    for i, (shape, dtype) in enumerate(_OUTS):
        dt = _mybir.dt.from_np(_np.dtype(dtype))
        args.append(nc.dram_tensor(f"out_{i}_dram", shape, dt, kind="ExternalOutput").ap())
    hybrid_trunk(nc, *args)
    r = _run(nc, [arrays], core_ids=[0])
    got = tuple(r.results[0][f"out_{i}_dram"] for i in range(len(_OUTS)))
    return got[0]
```

```python
from contextlib import ExitStack

import concourse.bass as bass
from concourse import mybir

ALU = mybir.AluOpType
ACT = mybir.ActivationFunctionType
F32 = mybir.dt.float32
F32R = mybir.dt.float32r
I32 = mybir.dt.int32

P = 128
EPS = 1e-6
POOL_WINDOWS = (2, 4, 8, 16)
WARM_UP = 14

SLAB = 2048
WIDTH = 256
RAW = 3
RING = 6


def at(count, per, i):
    return count if i is None else i * per + count


def hybrid_trunk(nc, x, ffn1_norm, ffn1_w_in, ffn1_w_out, mix_norm, ffn2_norm, ffn2_w_in, ffn2_w_out,
                 ab_w_in, pool_w, pool_b, pool_scale, conv_w, conv_b, conv_ln_g, conv_ln_b, ab_w_out,
                 sgu_w_in, sgu_ln_g, sgu_ln_b, sgu_w, sgu_b, sgu_w_out, final_norm, out):
    _, T, D = x.shape
    TT = T // P
    KD = D // P
    FF = ffn1_w_out.shape[1]
    STEPS = FF // WIDTH
    POOL_CH = pool_scale.shape[1]
    CONV_CH = conv_b.shape[1]
    TAPS = conv_w.shape[1]
    CT = CONV_CH // P
    G = len(POOL_WINDOWS)
    HEADS = sgu_w.shape[1]
    HALF = D // 2
    assert TT == 2 and KD * WIDTH == SLAB and 2 * D == SLAB and STEPS == 11
    assert ffn1_norm.shape[0] == 2 and POOL_CH == G * P and CT == 4 and HEADS == 8 and G == 4

    FFN_SLABS, MIX0_SLABS, MIX1_SLABS = 3 * STEPS, 10, 12
    stages = [("ffn", ffn1_w_in[0], ffn1_w_out[0], ffn1_norm[0]), ("mix0", None, None, mix_norm[0]),
              ("ffn", ffn2_w_in[0], ffn2_w_out[0], ffn2_norm[0]),
              ("ffn", ffn1_w_in[1], ffn1_w_out[1], ffn1_norm[1]), ("mix1", None, None, mix_norm[1]),
              ("ffn", ffn2_w_in[1], ffn2_w_out[1], ffn2_norm[1])]
    gains = [s[3] for s in stages] + [final_norm]
    slabs_of = {"ffn": FFN_SLABS, "mix0": MIX0_SLABS, "mix1": MIX1_SLABS}
    banks_of = {"ffn": STEPS, "mix0": 4, "mix1": 4}
    base, fill0, ffn0 = [0], [0], [0]
    for kind, *_ in stages:
        base.append(base[-1] + slabs_of[kind])
        fill0.append(fill0[-1] + banks_of[kind])
        ffn0.append(ffn0[-1] + (STEPS if kind == "ffn" else 0))
    TOTAL = base[-1]

    order = []
    for k, (kind, *_) in enumerate(stages):
        order += [("norm", k, t, h) for t in range(TT) for h in range(2)]
        if kind != "mix1":
            order += [("hidden", k)]
        if k == 0:
            order += ["taps", "columns"]
        if kind == "mix0":
            order += [("pooled", 0), ("pooled", 1), ("pool", 0), ("pool", 1), "var", "spread"]
        if kind == "mix1":
            order += [("spatial_w", 0), ("spatial_w", 1)] + [("spatial", j) for j in range(4)]
    small = {name: n for n, name in enumerate(order)}

    with ExitStack() as ctx:
        def sb(name, shape, dt=F32):
            return ctx.enter_context(nc.sbuf_tensor(name, shape, dt))

        def sem(name):
            return ctx.enter_context(nc.semaphore(name))

        raw = sb("raw", [P, RAW, SLAB])
        w_hi = sb("w_hi", [P, RING, SLAB], F32R)
        w_lo = sb("w_lo", [P, RING, SLAB], F32R)
        xres = sb("xres", [P, TT, D])
        xs = sb("xs", [P, TT, D])
        xn_hi = sb("xn_hi", [P, KD, T], F32R)
        xn_lo = sb("xn_lo", [P, KD, T], F32R)
        act_hi = sb("act_hi", [P, KD, T], F32R)
        act_lo = sb("act_lo", [P, KD, T], F32R)
        sgh = sb("sgh", [P, 2, 2, T])
        gain = sb("gain", [P, 2, D])
        scratch = sb("scratch", [P, 6144])
        ident = sb("ident", [P, P])
        ones = sb("ones", [P, P])
        avg = sb("avg", [P, P])
        ms = sb("ms", [P, TT, 2])
        ms_eps = sb("ms_eps", [P, TT])
        rstd = sb("rstd", [P, TT])
        minus_half = sb("minus_half", [P, TT])
        cnt_i = sb("cnt_i", [P, 16], I32)
        share = sb("share", [P, G, 16])
        pool_bias = sb("pool_bias", [P, G])
        warm = sb("warm", [P, 1])
        taps = sb("taps", [P, CT, TAPS])
        cols = sb("cols", [P, 5, CT])
        stats = sb("stats", [P, TT, 4, 6])
        mv = sb("mv", [P, TT, 2])
        ROOTS = 2 * (len(stages) + 1) + 2
        CONSTS = 11
        ga = ctx.enter_context(nc.psum_tensor("ga", [P, 2, T], F32))
        ub = ctx.enter_context(nc.psum_tensor("ub", [P, 2, T], F32))
        acc = [[ctx.enter_context(nc.psum_tensor(f"acc{t}{h}", [P, HALF], F32)) for h in range(2)]
               for t in range(TT)]
        tp = [ctx.enter_context(nc.psum_tensor(f"tp{b}", [P, 512], F32)) for b in range(2)]

        LEAD = TAPS - 1
        o = 0

        def space(n, rows=P):
            nonlocal o
            o += n
            assert o <= scratch.shape[1]
            return scratch[0:rows, o - n:o]

        u = space(TT * POOL_CH).rearrange("p (t c) -> p t c", t=TT)
        mixed = u.rearrange("p t c -> p (t c)").rearrange("p (g t) -> p g t", g=G)
        pooled = space(G * T).rearrange("p (g t) -> p g t", g=G)
        conv_in = space(CT * (LEAD + T)).rearrange("p (c t) -> p c t", c=CT)
        pw = space(G * P).rearrange("p (g d) -> p g d", g=G)
        tap_rows = space(CONV_CH, TAPS)
        col_rows = space(P, 5 * CT)
        window = space(G * 3 * P).rearrange("p (g b t) -> p g b t", g=G, b=3)
        diag = space(T)
        y = xs[:, 0, :].rearrange("p (c t) -> p c t", c=CT)
        yc = xs[:, 1, :].rearrange("p (c t) -> p c t", c=CT)
        sq = sgh[:, :, :, :].rearrange("p a b t -> p (a b) t")
        SHARED = 16
        pe_taps = [(CT - 1, q) for q in range(TAPS)] + [(CT - 2, q) for q in range(TAPS - SHARED, TAPS)]
        DIAGS = 2 * D // P

        def tap_diag(m):
            half, o = m % DIAGS // KD, m % KD * P
            return (xs if half == 0 else gain)[:, 1, o:o + P]

        uT = scratch[:, 0:KD * T].rearrange("p (k t) -> p k t", k=KD)
        ln_g = scratch[:, 2048:2048 + D]
        ln_b = scratch[:, 3072:3072 + D]
        sb_rep = scratch[:, 4096:4096 + HEADS * P].rearrange("p (h s) -> p h s", h=HEADS)
        spatial_wT = scratch[:, 5120:5120 + HEADS * P].rearrange("p (h s) -> p h s", h=HEADS)
        spatial_w = sgh[:, :, :, :].rearrange("p a b t -> p (a b t)").rearrange("p (h s) -> p h s", h=HEADS)

        x_landed = [sem(f"x_landed{t}") for t in range(TT)]
        gain_landed = [sem(f"gain_landed{i}") for i in range(2)]
        mix0_landed = sem("mix0_landed")
        mix1_landed = sem("mix1_landed")
        spatial_landed = sem("spatial_landed")
        raw_landed = [sem(f"raw_landed{i}") for i in range(RAW)]
        hi_half = sem("hi_half")
        lo_half = sem("lo_half")
        hi_split = sem("hi_split")
        lo_split = sem("lo_split")
        slab_used = sem("slab_used")
        first_out = sem("first_out")
        ga_free = sem("ga_free")
        ub_free = sem("ub_free")
        h_hi_done = sem("h_hi_done")
        h_done = sem("h_done")
        consts = sem("consts")
        share_done = sem("share_done")
        pool_step = sem("pool_step")
        window_done = sem("window_done")
        x_ready = sem("x_ready")
        ms_ready = sem("ms_ready")
        eps_ready = sem("eps_ready")
        rstd_ready = sem("rstd_ready")
        xs_ready = sem("xs_ready")
        small_full = sem("small_full")
        small_free = sem("small_free")
        xn_hi_ready = sem("xn_hi_ready")
        dve_step = sem("dve_step")
        conv_step = sem("conv_step")
        tap_built = sem("tap_built")
        tap_used = sem("tap_used")
        mean_full = sem("mean_full")
        yc_ready = sem("yc_ready")
        cols_ready = sem("cols_ready")
        mixed_ready = sem("mixed_ready")
        mix_hi = sem("mix_hi")
        mix_ready = sem("mix_ready")
        sq_ready = sem("sq_ready")
        diag_ready = sem("diag_ready")
        yn_ready = sem("yn_ready")
        post_ready = sem("post_ready")
        mask_ready = sem("mask_ready")
        v_ready = sem("v_ready")
        gu_ready = sem("gu_ready")
        gu_hi = sem("gu_hi")
        gu_done = sem("gu_done")
        half_out = sem("half_out")
        gained = sem("gained")
        scaled = [sem(f"scaled{h}") for h in range(2)]
        out_landed = sem("out_landed")

        block = ctx.enter_context(nc.Block())

        @block.sync
        def _(sp):
            def load(n, src, i=None):
                if n >= RAW or i is not None:
                    sp.wait_ge(lo_split, at(n - RAW + 1, RING, i))
                sp.dma_start(raw[:, n % RAW, :].rearrange("p (c n) -> p c n", n=src.shape[-1]), src)\
                    .then_inc(raw_landed[n % RAW], 16)

            def gain_load(k):
                if k >= 2:
                    sp.wait_ge(xs_ready, 4 * (k - 1))
                if k == 3:
                    sp.wait_ge(slab_used, base[2])
                sp.dma_start(gain[:, k % 2, :], gains[k].rearrange("(a d) -> a d", a=1).broadcast_to([P, D]))\
                    .then_inc(gain_landed[k % 2], 16)

            def in_view(w):
                return w.rearrange("(c p) n -> p c n", p=P)

            def out_view(w):
                return w.rearrange("(c p) n -> p c n", p=P)

            sp.dma_start(xres[:, 0, :], x[0, 0:P, :]).then_inc(x_landed[0], 16)

            for k, (kind, w_in, w_out, _) in enumerate(stages):
                b = base[k]
                if kind == "ffn":
                    wi, wo = in_view(w_in), out_view(w_out)
                    if k == 0:
                        gain_load(0)
                    load(b, wi[:, :, 0:WIDTH])
                    if k == 0:
                        for t in range(1, TT):
                            sp.dma_start(xres[:, t, :], x[0, t * P:(t + 1) * P, :]).then_inc(x_landed[t], 16)
                    load(b + 1, wi[:, :, FF:FF + WIDTH])
                    def turn(i, run):
                        for j in range(2):
                            n, s = b + 2 + 3 * j, 1 + j
                            load(n, wi[:, :, bass.ds(i * (2 * WIDTH) + s * WIDTH, WIDTH)], run)
                            load(n + 1, wi[:, :, bass.ds(i * (2 * WIDTH) + (FF + s * WIDTH), WIDTH)], run)
                            load(n + 2, wo[:, bass.ds(i * 4 + 2 * (s - 1), 2), :], run)

                    turn(0, None)
                    if k == 0:
                        sp.dma_start(pw, pool_w[0].rearrange("g c d -> c g d")).then_inc(mix0_landed, 16)
                        sp.dma_start(tap_rows, conv_w[0]).then_inc(mix0_landed, 16)
                        rows = [pool_b[0], pool_scale[0].rearrange("(c p) -> c p", p=P),
                                conv_b[0].rearrange("(c p) -> c p", p=P),
                                conv_ln_g[0].rearrange("(c p) -> c p", p=P),
                                conv_ln_b[0].rearrange("(c p) -> c p", p=P)]
                        for r, src in enumerate(rows):
                            sp.dma_start(col_rows[r * CT:(r + 1) * CT, :], src).then_inc(mix0_landed, 16)
                    with sp.Fori(1, (STEPS - 3) // 2) as i:
                        turn(i, i)
                    if k == 2:
                        sp.wait_ge(slab_used, base[2])
                        sp.dma_start(ln_g, sgu_ln_g[0].rearrange("(a d) -> a d", a=1).broadcast_to([P, D]))\
                            .then_inc(mix1_landed, 16)
                        sp.dma_start(ln_b, sgu_ln_b[0].rearrange("(a d) -> a d", a=1).broadcast_to([P, D]))\
                            .then_inc(mix1_landed, 16)
                        sp.dma_start(scratch[:, 4096:4096 + HEADS * P],
                                     sgu_b[0].rearrange("(a h) s -> a (h s)", a=1).broadcast_to([P, HEADS * P]))\
                            .then_inc(mix1_landed, 16)
                    n = b + 2 + 3 * (STEPS - 3)
                    for s in (STEPS - 2, STEPS - 1):
                        load(n, wi[:, :, s * WIDTH:(s + 1) * WIDTH])
                        load(n + 1, wi[:, :, FF + s * WIDTH:FF + (s + 1) * WIDTH])
                        n += 2
                    for s in range(STEPS - 3, STEPS):
                        load(n, wo[:, 2 * s:2 * s + 2, :])
                        n += 1
                elif kind == "mix0":
                    wi, wo = in_view(ab_w_in[0]), out_view(ab_w_out[0])
                    gate, a = POOL_CH + CONV_CH, POOL_CH
                    for j, c in enumerate((gate, a, gate + WIDTH, a + WIDTH, 0, WIDTH)):
                        load(b + j, wi[:, :, c:c + WIDTH])
                    for j in range(4):
                        load(b + 6 + j, wo[:, 2 * j:2 * j + 2, :])
                else:
                    wi, wo = in_view(sgu_w_in[0]), out_view(sgu_w_out[0])
                    for j in range(8):
                        c = (D + j * WIDTH) if j < 4 else (j - 4) * WIDTH
                        load(b + j, wi[:, :, c:c + WIDTH])
                    sp.wait_ge(slab_used, b)
                    sp.dma_start(spatial_w, sgu_w[0].rearrange("h s t -> s h t"))\
                        .then_inc(spatial_landed, 16)
                    for j in range(4):
                        load(b + 8 + j, wo[:, 2 * j:2 * j + 2, :])
                gain_load(k + 1)

            for t in range(TT):
                for h in range(2):
                    sp.wait_ge(scaled[h], t + 1)
                    sp.dma_start(out[0, t * P:(t + 1) * P, h * HALF:(h + 1) * HALF],
                                 xs[:, t, h * HALF:(h + 1) * HALF]).then_inc(out_landed, 16)
            sp.wait_ge(out_landed, 16 * 2 * TT)

        @block.gpsimd
        def _(pool):
            pool.memset(minus_half[:, :], -0.5).then_inc(consts, 1)
            pool.memset(ident[:, :], 0.0).then_inc(consts, 1)
            pool.memset(ones[:, :], 1.0).then_inc(consts, 1)
            pool.memset(avg[:, :], 1.0 / CONV_CH).then_inc(consts, 1)
            for g, w in enumerate(POOL_WINDOWS):
                pool.memset(window[:, g, :, :], 1.0 / w).then_inc(consts, 1)
            pool.memset(conv_in[:, :, 0:LEAD], 0.0).then_inc(consts, 1)
            pool.iota(cnt_i[:, :], pattern=[[1, 16]], base=1, channel_multiplier=0).then_inc(consts, 1)
            pool.wait_ge(consts, CONSTS - 1)
            pool.affine_select(out=ident[:, :], in_=ident[:, :], compare_op=ALU.not_equal, fill=1.0,
                               base=0, pattern=[[-1, P]], channel_multiplier=1).then_inc(consts, 1)

            def windows():
                pool.wait_ge(share_done, G + 2)
                n = 0
                for lo, hi in ((0, 2), (2, 3)):
                    part = window[:, :, lo:hi, :].rearrange("p g b t -> p g (b t)")
                    pool.affine_select(out=part, in_=part, compare_op=ALU.is_ge, fill=0.0, base=0,
                                       pattern=[[0, G], [1, (hi - lo) * P]], channel_multiplier=-1)\
                        .then_inc(pool_step, 1)
                    n += 1
                pool.wait_ge(pool_step, n)
                for lo, hi in ((0, 2), (2, 3)):
                    for g, w in enumerate(POOL_WINDOWS):
                        part = window[:, g, lo:hi, :].rearrange("p b t -> p (b t)")
                        pool.affine_select(out=part, in_=part, compare_op=ALU.is_ge, fill=0.0, base=w - 1,
                                           pattern=[[-1, (hi - lo) * P]], channel_multiplier=1)\
                            .then_inc(pool_step, 1)
                        n += 1
                pool.wait_ge(pool_step, n)
                pool.wait_ge(consts, CONSTS)
                same = ident[:, :].rearrange("p (g t) -> p g t", g=1).broadcast_to([P, G, P])
                for block in (0, 2):
                    pool.tensor_tensor(window[:, :, block, :], window[:, :, block, :], same, ALU.subtract)\
                        .then_inc(window_done, 1)

            seen = 0

            def root(lo, hi):
                nonlocal seen
                seen += 1
                pool.wait_ge(eps_ready, seen)
                pool.tensor_tensor(rstd[:, lo:hi], ms_eps[:, lo:hi], minus_half[:, lo:hi], ALU.pow)\
                    .then_inc(rstd_ready, 1)

            for k in range(len(stages) + 1):
                for t in range(TT):
                    root(t, t + 1)
                if k == 0:
                    windows()
                kind = stages[k][0] if k < len(stages) else None
                if kind == "mix0":
                    root(0, TT)
                if kind == "mix1":
                    pool.wait_ge(spatial_landed, 16)
                    pool.affine_select(out=spatial_w, in_=spatial_w, compare_op=ALU.is_ge, fill=0.0, base=0,
                                       pattern=[[0, HEADS], [-1, P]], channel_multiplier=1)\
                        .then_inc(mask_ready, 1)
                    root(0, TT)

        @block.scalar
        def _(act):
            nxt = 0

            def split(n, i=None):
                act.wait_ge(raw_landed[n % RAW], at(16 * (n // RAW + 1), 16 * RING // RAW, i))
                if n >= RING:
                    act.wait_ge(slab_used, at(n - RING + 1, RING, i))
                o = 0
                if n == 0:
                    o = SLAB // 2
                    act.activation(w_hi[:, 0, 0:o], raw[:, 0, 0:o], ACT.Copy).then_inc(hi_half, 1)
                act.activation(w_hi[:, n % RING, o:], raw[:, n % RAW, o:], ACT.Copy).then_inc(hi_split, 1)

            def split_to(n):
                nonlocal nxt
                while nxt <= min(n, TOTAL - 1):
                    split(nxt)
                    nxt += 1

            def norm(k, t):
                for h in range(2):
                    if k == 0:
                        act.wait_ge(x_landed[t], 16)
                    else:
                        act.wait_ge(x_ready, 4 * (k - 1) + 2 * t + h + 1)
                    act.activation(xs[:, t, h * HALF:(h + 1) * HALF], xres[:, t, h * HALF:(h + 1) * HALF],
                                   ACT.Square, scale=float(D) ** -0.5,
                                   accum_out=ms[:, t, h:h + 1]).then_inc(ms_ready, 1)
                if k == 0 and t == 1:
                    split_to(1)
                for h in range(2):
                    n = small[("norm", k, t, h)]
                    act.wait_ge(small_full, n + 1)
                    act.activation(xn_hi[:, 4 * h:4 * h + 4, t * P:(t + 1) * P],
                                   tp[n % 2][:, :].rearrange("p (c t) -> p c t", c=4), ACT.Copy)\
                        .then_inc(xn_hi_ready, 1)

            def final(t):
                last = len(stages)
                for h in range(2):
                    act.wait_ge(x_ready, 4 * (last - 1) + 2 * t + h + 1)
                    c, o = slice(h * HALF, (h + 1) * HALF), (2 * t + h) * HALF
                    act.activation(scratch[:, o:o + HALF], xres[:, t, c], ACT.Square, scale=float(D) ** -0.5,
                                   accum_out=ms[:, t, h:h + 1]).then_inc(ms_ready, 1)
                act.wait_ge(gained, 2 * t + 2)
                act.wait_ge(rstd_ready, ROOTS - 1 + t)
                act.activation(xs[:, t, HALF:], xs[:, t, HALF:], ACT.Copy, scale=rstd[:, t:t + 1])\
                    .then_inc(scaled[1], 1)

            def gate(n, f, func, i=None, per=2):
                act.wait_ge(slab_used, at(n + 1, RING, i))
                if f:
                    act.wait_ge(ub_free, at(f, per, i))
                act.activation(sgh[:, 0, :, :], ga[:, :, :], func).then_inc(ga_free, 1)

            def product_hi(slot, f, i=None):
                act.wait_ge(ub_free, at(f + 1, 2, i))
                act.activation(act_hi[:, 2 * slot:2 * slot + 2, :], sgh[:, 1, :, :], ACT.Copy)\
                    .then_inc(h_hi_done, 1)

            for k, (kind, *_) in enumerate(stages):
                b, f = base[k], fill0[k]
                norm(k, 0)
                split_to(b)
                norm(k, 1)
                split_to(b + 3)
                if kind == "ffn":
                    gate(b, f, ACT.Silu)
                    split_to(b + 5)
                    n = small[("hidden", k)]
                    act.wait_ge(small_full, n + 1)
                    act.activation(act_hi[:, 0:2, :], tp[n % 2][:, :].rearrange("p (j t) -> p j t", j=2), ACT.Copy)\
                        .then_inc(h_hi_done, 1)
                    split_to(b + 7)
                    with act.Fori(0, (STEPS - 3) // 2) as i:
                        for j in range(2):
                            n, s = b + 2 + 3 * j, 1 + j
                            gate(n, f + s, ACT.Silu, i)
                            split(n + 6, i)
                            product_hi(s % 2, f + s, i)
                            split(n + 7, i)
                            split(n + 8, i)
                    nxt += 3 * (STEPS - 3)
                    n = b + 2 + 3 * (STEPS - 3)
                    for s in (STEPS - 2, STEPS - 1):
                        gate(n, f + s, ACT.Silu)
                        split_to(n + 6)
                        product_hi(1 if s == STEPS - 2 else 2, f + s)
                        split_to(n + 7)
                        n += 2
                elif kind == "mix0":
                    gate(b, f, ACT.Sigmoid)
                    split_to(b + 4)
                    n = small[("hidden", k)]
                    act.wait_ge(small_full, n + 1)
                    act.wait_ge(consts, CONSTS)
                    act.activation(conv_in[:, 0:2, LEAD:], tp[n % 2][:, :].rearrange("p (j t) -> p j t", j=2),
                                   ACT.Copy).then_inc(small_free, 1)
                    split_to(b + 5)

                    def build_taps(lo, hi):
                        for m in range(lo, hi):
                            if m >= DIAGS:
                                act.wait_ge(tap_used, m - DIAGS + 1)
                            c, q = pe_taps[m]
                            act.activation(tap_diag(m), ident[:, :], ACT.Copy, scale=taps[:, c, q:q + 1])\
                                .then_inc(tap_built, 1)

                    gate(b + 2, f + 1, ACT.Sigmoid)
                    act.wait_ge(cols_ready, 1)
                    build_taps(0, DIAGS)
                    split_to(b + 6)
                    for j, (bank, free) in enumerate(((ga, ga_free), (ub, ub_free))):
                        act.wait_ge(slab_used, b + 5 + j)
                        act.activation(u[:, :, j * WIDTH:(j + 1) * WIDTH], bank[:, :, :], ACT.Copy)\
                            .then_inc(free, 1)
                        split_to(b + 7 + j)
                    act.activation(warm[:, :], ident[:, 0:1], ACT.Silu)
                    build_taps(DIAGS, TAPS)
                    for j in range(2):
                        n = small[("pooled", j)]
                        act.wait_ge(small_full, n + 1)
                        act.activation(pooled[:, 2 * j:2 * j + 2, :],
                                       tp[n % 2][:, :].rearrange("p (g t) -> p g t", g=2), ACT.Copy)\
                            .then_inc(small_free, 1)
                    build_taps(TAPS, TAPS + 8)
                    for j in range(2):
                        n = small[("pool", j)]
                        act.wait_ge(small_full, n + 1)
                        for a, done in ((0, mixed_ready), (1, small_free)):
                            g = 2 * j + a
                            act.activation(mixed[:, g, :], tp[n % 2][:, a * T:(a + 1) * T], ACT.Identity,
                                           bias=pool_bias[:, g:g + 1], scale=cols[:, 1, g:g + 1]).then_inc(done, 1)
                        act.wait_ge(mixed_ready, j + 1)
                        act.wait_ge(small_free, n + 1)
                        act.activation(act_hi[:, 2 * j:2 * j + 2, :], mixed[:, 2 * j:2 * j + 2, :], ACT.Copy)\
                            .then_inc(mix_hi, 1)
                    split_to(b + 9)
                    build_taps(TAPS + 8, len(pe_taps))
                    act.wait_ge(tap_used, TAPS)
                    act.activation(y[:, CT - 1, :], ga[:, 0, :], ACT.Identity, bias=cols[:, 2, CT - 1:CT])\
                        .then_inc(ga_free, 1)
                    for j in range(2):
                        act.wait_ge(yc_ready, j + 1)
                        act.activation(sq[:, 2 * j:2 * j + 2, :], yc[:, 2 * j:2 * j + 2, :], ACT.Square)\
                            .then_inc(sq_ready, 1)
                    split_to(b + 10)
                    for c in range(CT):
                        if c < 2:
                            act.wait_ge(yn_ready, 1)
                        else:
                            act.wait_ge(small_free, small["spread"] + 1)
                        act.activation(sq[:, c, :], y[:, c, :], ACT.Silu, bias=cols[:, 4, c:c + 1],
                                       scale=cols[:, 3, c:c + 1]).then_inc(post_ready, 1)
                        if c % 2:
                            act.wait_ge(post_ready, c + 1)
                            act.activation(act_hi[:, 3 + c:5 + c, :], sq[:, c - 1:c + 1, :], ACT.Copy)\
                                .then_inc(mix_hi, 1)
                    split_to(b + 11)
                else:
                    for j in range(4):
                        bank, free = ((ga, ga_free), (ub, ub_free))[j % 2]
                        act.wait_ge(slab_used, b + j + 1)
                        act.wait_ge(small_full, small[("norm", k, 1, 1)] + 1)
                        act.activation(xs[:, :, j * WIDTH:(j + 1) * WIDTH], bank[:, :, :], ACT.Gelu)\
                            .then_inc(free, 1)
                        split_to(b + (4, 7, 8, 9)[j])
                    act.wait_ge(mix1_landed, 16 * 3)
                    for j in range(4):
                        bank, free = ((ga, ga_free), (ub, ub_free))[j % 2]
                        act.wait_ge(slab_used, b + 5 + j)
                        act.activation(uT[:, 2 * j:2 * j + 2, :], bank[:, :, :], ACT.Gelu).then_inc(free, 1)
                        split_to(b + (10, 11, 11, 12)[j])
                        if j >= 2:
                            for g in (2 * j - 4, 2 * j - 3):
                                act.wait_ge(gu_ready, g + 1)
                                act.activation(act_hi[:, 2 * g:2 * g + 2, :], uT[:, 2 * g:2 * g + 2, :], ACT.Copy)\
                                    .then_inc(gu_hi, 1)
                    split_to(b + 13)
            for t in range(TT):
                final(t)

        @block.vector
        def _(dve):
            nxt = 0
            steps = 0
            roots = 0
            tsplit = []

            def split(n, i=None):
                o = 0
                if n == 0:
                    o = SLAB // 2
                    dve.wait_ge(hi_half, 1)
                    dve.tensor_tensor(w_lo[:, 0, 0:o], raw[:, 0, 0:o], w_hi[:, 0, 0:o].bitcast(F32),
                                      ALU.subtract).then_inc(lo_half, 1)
                dve.wait_ge(hi_split, at(n + 1, RING, i))
                dve.tensor_tensor(w_lo[:, n % RING, o:], raw[:, n % RAW, o:], w_hi[:, n % RING, o:].bitcast(F32),
                                  ALU.subtract).then_inc(lo_split, 1)

            def split_to(n):
                nonlocal nxt
                while nxt <= min(n, TOTAL - 1):
                    split(nxt)
                    nxt += 1

            def own(instruction):
                nonlocal steps
                steps += 1
                instruction.then_inc(dve_step, 1)
                return steps

            def root_wait(value):
                nonlocal roots
                roots += 1
                value.then_inc(eps_ready, 1)
                dve.wait_ge(rstd_ready, roots)

            def norm(k, t):
                if k:
                    scale = 0.5 if stages[k - 1][0] == "ffn" else 1.0
                    if t == 0:
                        dve.wait_ge(first_out, k)
                    else:
                        dve.wait_ge(slab_used, base[k])
                    for h in range(2):
                        xh = xres[:, t, h * HALF:(h + 1) * HALF]
                        dve.scalar_tensor_tensor(out=xh, in0=acc[t][h][:, :], scalar=scale, in1=xh,
                                                 op0=ALU.mult, op1=ALU.add).then_inc(x_ready, 1)
                dve.wait_ge(ms_ready, 4 * k + 2 * t + 2)
                root_wait(dve.tensor_scalar(ms_eps[:, t:t + 1], ms[:, t, 0:1], ms[:, t, 1:2], EPS,
                                            ALU.add, ALU.add))
                dve.wait_ge(gain_landed[k % 2], 16 * (k // 2 + 1))
                for h in range(2):
                    c = slice(h * HALF, (h + 1) * HALF)
                    dve.scalar_tensor_tensor(out=xs[:, t, c], in0=xres[:, t, c], scalar=rstd[:, t:t + 1],
                                             in1=gain[:, k % 2, c], op0=ALU.mult, op1=ALU.mult)\
                        .then_inc(xs_ready, 1)
                for h in range(2):
                    n = small[("norm", k, t, h)]
                    dve.wait_ge(xn_hi_ready, 4 * k + 2 * t + h + 1)
                    hi = xn_hi[:, 4 * h:4 * h + 4, t * P:(t + 1) * P]
                    dve.tensor_tensor(xn_lo[:, 4 * h:4 * h + 4, t * P:(t + 1) * P],
                                      tp[n % 2][:, :].rearrange("p (c t) -> p c t", c=4),
                                      hi.bitcast(F32), ALU.subtract).then_inc(small_free, 1)

            def final(t):
                last = len(stages)
                if t == 0:
                    dve.wait_ge(first_out, last)
                for h in range(2):
                    if t == 1:
                        if h == 0:
                            dve.wait_ge(half_out, 1)
                        else:
                            dve.wait_ge(slab_used, base[last])
                    xh = xres[:, t, h * HALF:(h + 1) * HALF]
                    dve.scalar_tensor_tensor(out=xh, in0=acc[t][h][:, :], scalar=0.5, in1=xh,
                                             op0=ALU.mult, op1=ALU.add).then_inc(x_ready, 1)
                dve.wait_ge(gain_landed[last % 2], 16 * (last // 2 + 1))
                for h in range(2):
                    dve.wait_ge(x_ready, 4 * (last - 1) + 2 * t + h + 1)
                    c = slice(h * HALF, (h + 1) * HALF)
                    dve.tensor_tensor(xs[:, t, c], xres[:, t, c], gain[:, last % 2, c], ALU.mult)\
                        .then_inc(gained, 1)
                dve.wait_ge(ms_ready, 4 * last + 2 * t + 2)
                root_wait(dve.tensor_scalar(ms_eps[:, t:t + 1], ms[:, t, 0:1], ms[:, t, 1:2], EPS,
                                            ALU.add, ALU.add))
                dve.wait_ge(gained, 2 * t + 1)
                dve.tensor_scalar(xs[:, t, 0:HALF], xs[:, t, 0:HALF], rstd[:, t:t + 1], None, ALU.mult)\
                    .then_inc(scaled[0], 1)

            def product(n, f, e=0, i=None, out=None):
                if e:
                    dve.wait_ge(h_done, at(e, 2, i))
                dve.wait_ge(slab_used, at(n + 1, RING, i))
                dve.wait_ge(ga_free, at(f + 1, 2, i))
                dve.tensor_tensor(sgh[:, 1, :, :] if out is None else out, ub[:, :, :], sgh[:, 0, :, :],
                                  ALU.mult).then_inc(ub_free, 1)

            def product_lo(slot, e, i=None):
                dve.wait_ge(h_hi_done, at(e + 1, 2, i))
                dve.tensor_tensor(act_lo[:, 2 * slot:2 * slot + 2, :], sgh[:, 1, :, :],
                                  act_hi[:, 2 * slot:2 * slot + 2, :].bitcast(F32), ALU.subtract)\
                    .then_inc(h_done, 1)

            def shares():
                dve.wait_ge(consts, CONSTS - 1)
                for g, w in enumerate(POOL_WINDOWS):
                    dve.tensor_scalar(share[:, g, :], cnt_i[:, :], float(w), None, ALU.min)\
                        .then_inc(share_done, 1)
                dve.wait_ge(share_done, G)
                dve.reciprocal(share[:, :, :], share[:, :, :]).then_inc(share_done, 1)
                dve.wait_ge(share_done, G + 1)
                dve.tensor_copy(window[:, :, 0, 0:16], share[:, :, :]).then_inc(share_done, 1)

            for k, (kind, *_) in enumerate(stages):
                b, f, e = base[k], fill0[k], ffn0[k]
                norm(k, 0)
                split_to(b)
                norm(k, 1)
                split_to(b + 3)
                if k == 0:
                    shares()
                if kind == "ffn":
                    split_to(b + 4)
                    product(b + 1, f, e)
                    split_to(b + 5)
                    n = small[("hidden", k)]
                    dve.wait_ge(h_hi_done, e + 1)
                    dve.tensor_tensor(act_lo[:, 0:2, :], tp[n % 2][:, :].rearrange("p (j t) -> p j t", j=2),
                                      act_hi[:, 0:2, :].bitcast(F32), ALU.subtract).then_inc(h_done, 1)
                    dve.wait_ge(h_done, e + 1)
                    dve.engine_nop().then_inc(small_free, 1)
                    split_to(b + 7)
                    with dve.Fori(0, (STEPS - 3) // 2) as i:
                        for j in range(2):
                            n, s = b + 2 + 3 * j, 1 + j
                            split(n + 6, i)
                            product(n + 1, f + s, e + s, i)
                            product_lo(s % 2, e + s, i)
                            split(n + 7, i)
                            split(n + 8, i)
                    nxt += 3 * (STEPS - 3)
                    n = b + 2 + 3 * (STEPS - 3)
                    for s in (STEPS - 2, STEPS - 1):
                        split_to(n + 6)
                        product(n + 1, f + s, e + s)
                        product_lo(1 if s == STEPS - 2 else 2, e + s)
                        split_to(n + 7)
                        n += 2
                    if k == 0:
                        n = small["taps"]
                        dve.wait_ge(small_full, n + 1)
                        dve.tensor_copy(taps[:, :, :],
                                        tp[n % 2][:, 0:CT * TAPS].rearrange("p (c k) -> p c k", c=CT))\
                            .then_inc(small_free, 1)
                        n = small["columns"]
                        dve.wait_ge(small_full, n + 1)
                        dve.tensor_copy(cols[:, :, :], tp[n % 2][:, 0:5 * CT].rearrange("p (r c) -> p r c", c=CT))\
                            .then_inc(small_free, 1)
                        dve.wait_ge(small_free, n + 1)
                        dve.tensor_tensor(pool_bias[:, :], cols[:, 0, :], cols[:, 1, :], ALU.mult)\
                            .then_inc(cols_ready, 1)
                elif kind == "mix0":
                    product(b + 1, f, e)
                    split_to(b + 4)
                    added = 0
                    done = {c: 0 for c in range(CT - 1)}
                    last = {}

                    def tap(c):
                        nonlocal added
                        q = done[c]
                        if q == 0:
                            ins = dve.tensor_scalar(y[:, c, :], conv_in[:, c, 0:T], taps[:, c, 0:1],
                                                    cols[:, 2, c:c + 1], ALU.mult, ALU.add)
                        else:
                            dve.wait_ge(conv_step, last[c])
                            ins = dve.scalar_tensor_tensor(out=y[:, c, :], in0=conv_in[:, c, q:q + T],
                                                           scalar=taps[:, c, q:q + 1], in1=y[:, c, :],
                                                           op0=ALU.mult, op1=ALU.add)
                        ins.then_inc(conv_step, 1)
                        added += 1
                        done[c], last[c] = q + 1, added

                    dve.wait_ge(small_free, small[("hidden", k)] + 1)
                    for q in range(5):
                        tap(0)
                        tap(1)
                    product(b + 3, f + 1, out=conv_in[:, 2:4, LEAD:])
                    split_to(b + 5)
                    dve.wait_ge(ub_free, f + 2)
                    for q in range(5, TAPS):
                        for c in (0, 2, 1) if q - 5 < TAPS - SHARED else (0, 1):
                            tap(c)
                        if q in (8, 12, 16):
                            split_to(b + 6 + (q - 8) // 4)
                        if q in (19, 21):
                            j = (q - 19) // 2
                            dve.wait_ge(mix_hi, j + 1)
                            dve.tensor_tensor(act_lo[:, 2 * j:2 * j + 2, :], mixed[:, 2 * j:2 * j + 2, :],
                                              act_hi[:, 2 * j:2 * j + 2, :].bitcast(F32), ALU.subtract)\
                                .then_inc(mix_ready, 1)
                    dve.wait_ge(tap_used, len(pe_taps))
                    dve.wait_ge(conv_step, last[2])
                    dve.tensor_tensor(y[:, 2, :], ub[:, 1, :], y[:, 2, :], ALU.add).then_inc(conv_step, 1)
                    dve.wait_ge(mean_full, 1)
                    mean = ub[:, 0:1, :].broadcast_to([P, 2, T])
                    for j in range(2):
                        dve.tensor_tensor(yc[:, 2 * j:2 * j + 2, :], y[:, 2 * j:2 * j + 2, :], mean, ALU.subtract)\
                            .then_inc(yc_ready, 1)
                    dve.wait_ge(yc_ready, 2)
                    dve.engine_nop().then_inc(ub_free, 1)
                    split_to(b + 9)
                    n = small["var"]
                    dve.wait_ge(small_full, n + 1)
                    dve.tensor_scalar(ms_eps[:, :], tp[n % 2][:, 0:TT], EPS, None, ALU.add)\
                        .then_inc(small_free, 1)
                    dve.wait_ge(small_free, n + 1)
                    root_wait(dve.engine_nop())
                    for t in range(TT):
                        dve.tensor_scalar(diag[:, t * P:(t + 1) * P], ident[:, :], rstd[:, t:t + 1], None,
                                          ALU.mult).then_inc(diag_ready, 1)
                    n = small["spread"]
                    dve.wait_ge(small_full, n + 1)
                    spread = tp[n % 2][:, 0:T].rearrange("p (a t) -> p a t", a=1).broadcast_to([P, 2, T])
                    for j, done in enumerate((yn_ready, small_free)):
                        dve.tensor_tensor(y[:, 2 * j:2 * j + 2, :], yc[:, 2 * j:2 * j + 2, :], spread, ALU.mult)\
                            .then_inc(done, 1)
                    for j in range(2):
                        dve.wait_ge(mix_hi, j + 3)
                        dve.tensor_tensor(act_lo[:, 4 + 2 * j:6 + 2 * j, :], sq[:, 2 * j:2 * j + 2, :],
                                          act_hi[:, 4 + 2 * j:6 + 2 * j, :].bitcast(F32), ALU.subtract)\
                            .then_inc(mix_ready, 1)
                    split_to(b + 11)
                else:
                    for j in range(4):
                        free = (ga_free, ub_free)[j % 2]
                        dve.wait_ge(free, f + j // 2 + 1)
                        for t in range(TT):
                            s = own(dve.bn_stats(stats[:, t, j, :], xs[:, t, j * WIDTH:(j + 1) * WIDTH]))
                        split_to(b + (4, 7, 8, 8)[j])
                    dve.wait_ge(dve_step, s)
                    for t in range(TT):
                        s = own(dve.bn_aggr(mv[:, t, :], stats[:, t, :, :].rearrange("p a b -> p (a b)")))
                    dve.wait_ge(dve_step, s)
                    root_wait(dve.tensor_scalar(ms_eps[:, :], mv[:, :, 1], EPS, None, ALU.add))
                    dve.wait_ge(mix1_landed, 16 * 3)
                    for t in range(TT):
                        s = own(dve.scalar_tensor_tensor(out=xs[:, t, :], in0=xs[:, t, :], scalar=mv[:, t, 0:1],
                                                         in1=ln_g, op0=ALU.subtract, op1=ALU.mult))
                    for t in range(TT):
                        dve.wait_ge(dve_step, s - 1 + t)
                        dve.scalar_tensor_tensor(out=xs[:, t, :], in0=xs[:, t, :], scalar=rstd[:, t:t + 1],
                                                 in1=ln_b, op0=ALU.mult, op1=ALU.add).then_inc(v_ready, 1)
                    for j in range(2):
                        n = small[("spatial_w", j)]
                        dve.wait_ge(small_full, n + 1)
                        dve.tensor_copy(spatial_wT[:, 4 * j:4 * j + 4, :],
                                        tp[n % 2][:, :].rearrange("p (h s) -> p h s", h=4)).then_inc(small_free, 1)
                    split_to(b + 9)
                    for half in range(2):
                        for j in (2 * half, 2 * half + 1):
                            n = small[("spatial", j)]
                            dve.wait_ge(small_full, n + 1)
                            tmp = sgh[:, j % 2, :, :]
                            bias = sb_rep[:, 2 * j:2 * j + 2, :].rearrange("p h (a s) -> p h a s", a=1)\
                                .broadcast_to([P, 2, TT, P])
                            dve.tensor_tensor(tmp.rearrange("p h (a s) -> p h a s", a=TT),
                                              tp[n % 2][:, :].rearrange("p (h a s) -> p h a s", h=2, a=TT),
                                              bias, ALU.add).then_inc(small_free, 1)
                            dve.wait_ge(small_free, n + 1)
                            dve.wait_ge((ga_free, ub_free)[j % 2], f + 2 + j // 2 + 1)
                            dve.tensor_tensor(uT[:, 2 * j:2 * j + 2, :], tmp, uT[:, 2 * j:2 * j + 2, :], ALU.mult)\
                                .then_inc(gu_ready, 1)
                        for j in (2 * half, 2 * half + 1):
                            dve.wait_ge(gu_hi, j + 1)
                            dve.tensor_tensor(act_lo[:, 2 * j:2 * j + 2, :], uT[:, 2 * j:2 * j + 2, :],
                                              act_hi[:, 2 * j:2 * j + 2, :].bitcast(F32), ALU.subtract)\
                                .then_inc(gu_done, 1)
                        split_to(b + 11 + 2 * half)
            for t in range(TT):
                final(t)

        @block.tensor
        def _(pe):
            def three(dst, s_hi, s_lo, m_hi, m_lo, start, stop):
                pe.matmul(dst, s_hi, m_hi, start=start, stop=False)
                pe.matmul(dst, s_hi, m_lo, start=False, stop=False)
                return pe.matmul(dst, s_lo, m_hi, start=False, stop=stop)

            def slab_ready(n, i=None):
                pe.wait_ge(lo_split, at(n + 1, RING, i))

            def slab_in(n, bank, between=None):
                for j in range(2):
                    if between is not None and j == 1:
                        between()
                    for c in range(KD):
                        o = c * WIDTH + j * P
                        mm = three(bank[:, j, :], w_hi[:, n % RING, o:o + P], w_lo[:, n % RING, o:o + P],
                                   xn_hi[:, c, :], xn_lo[:, c, :], c == 0, c == KD - 1)
                return mm

            def slab_in_rows(n, bank, t, fresh=None, between=None):
                tok = slice(t * P, (t + 1) * P)
                for c in range(KD):
                    if n == 0 and t == 0 and c == KD // 2:
                        slab_ready(0)
                    if fresh is not None and c % 4 == 0:
                        pe.wait_ge(small_free, fresh + c // 4 + 1)
                    if between is not None and c in between:
                        between[c]()
                    o = slice(c * WIDTH, (c + 1) * WIDTH)
                    mm = three(bank[:, t, :], xn_hi[:, c, tok], xn_lo[:, c, tok], w_hi[:, n % RING, o],
                               w_lo[:, n % RING, o], c == 0, c == KD - 1)
                return mm

            def slab_out(n, t, tile, start, stop, between=None, half=None):
                tok = slice(t * P, (t + 1) * P)
                for c in range(2):
                    if between is not None and c == 1:
                        between()
                    for h in range(2):
                        o = slice(c * D + h * HALF, c * D + (h + 1) * HALF)
                        mm = three(acc[t][h][:, :], act_hi[:, tile + c, tok], act_lo[:, tile + c, tok],
                                   w_hi[:, n % RING, o], w_lo[:, n % RING, o], start and c == 0, stop and c == 1)
                        if half is not None and (c, h) == (1, 0):
                            mm.then_inc(half, 1)
                return mm

            def small_bank(name):
                n = small[name]
                if n >= 2:
                    pe.wait_ge(small_free, n - 1)
                return tp[n % 2]

            def transposes(k, t, halves=(0, 1)):
                for h in halves:
                    bank = small_bank(("norm", k, t, h))
                    pe.wait_ge(xs_ready, 4 * k + 2 * t + h + 1)
                    for c in range(4):
                        o = h * HALF + c * P
                        mm = pe.transpose(bank[:, c * P:(c + 1) * P], xs[:, t, o:o + P], ident[:, :])
                    mm.then_inc(small_full, 1)

            def first_pair(k, f):
                b = base[k]
                pairs = [(t, a) for t in range(TT) for a in range(2)]
                if k == 0:
                    pairs.sort(key=lambda p: p[1])
                for t, a in pairs:
                    bank, free = ((ga, ga_free), (ub, ub_free))[a]
                    if t == 0:
                        if f:
                            pe.wait_ge(free, f)
                        if b + a:
                            slab_ready(b + a)
                        else:
                            pe.wait_ge(lo_half, 1)
                    between = None
                    if (t, a) == (0, 0 if k == 0 else 1):
                        between = {KD // 2: lambda: transposes(k, 1, (0,)), KD - 1: lambda: transposes(k, 1, (1,))}
                    mm = slab_in_rows(b + a, bank, t, small[("norm", k, t, 0)] if a == 0 else None, between)
                    if t == TT - 1:
                        mm.then_inc(slab_used, 1)

            def hidden(k, f):
                bank = small_bank(("hidden", k))
                pe.wait_ge(ub_free, f + 1)
                for j in range(2):
                    for t in range(TT):
                        o = j * T + t * P
                        mm = pe.transpose(bank[:, o:o + P], sgh[:, 1, t, j * P:(j + 1) * P], ident[:, :])
                mm.then_inc(small_full, 1)

            def open_bank(n, which, f, i=None, per=2):
                bank, free = ((ga, ga_free), (ub, ub_free))[which]
                slab_ready(n, i)
                pe.wait_ge(free, at(f, per, i))
                return bank

            def full_in(n, which, f, i=None, per=2):
                slab_in(n, open_bank(n, which, f, i, per)).then_inc(slab_used, 1)

            def tail(k, slabs, ready, start=None):
                for t in range(TT):
                    for a, (n, tile) in enumerate(slabs):
                        last = a == len(slabs) - 1
                        if t == 0:
                            slab_ready(n)
                            ready(a)
                        between = half = None
                        if last and t == TT - 1:
                            if k + 1 < len(stages):
                                between = lambda: transposes(k + 1, 0)
                            else:
                                half = half_out
                        mm = slab_out(n, t, tile, start == n, last, between, half)
                        if t == TT - 1:
                            mm.then_inc(slab_used, 1)
                    if t == 0:
                        mm.then_inc(first_out, 1)

            def warm_up(count):
                for _ in range(count):
                    pe.matmul(ga[:, 0, 0:P], ones[:, :], avg[:, :], start=True, stop=True)

            pe.wait_ge(consts, 4)
            warm_up(WARM_UP)
            pe.wait_ge(consts, CONSTS)
            transposes(0, 0)
            warm_up(WARM_UP)
            for k, (kind, *_) in enumerate(stages):
                b, f, e = base[k], fill0[k], ffn0[k]
                if kind == "ffn":
                    first_pair(k, f)

                    def step_out(n, slot, done, start, i=None):
                        slab_ready(n, i)
                        pe.wait_ge(h_done, at(done, 2, i))
                        for t in range(TT):
                            mm = slab_out(n, t, 2 * slot, start, False)
                        mm.then_inc(slab_used, 1)

                    full_in(b + 2, 0, f + 1)
                    hidden(k, f)
                    full_in(b + 3, 1, f + 1)
                    step_out(b + 4, 0, e + 1, True)
                    full_in(b + 5, 0, f + 2)
                    full_in(b + 6, 1, f + 2)
                    step_out(b + 7, 1, e + 2, False)
                    with pe.Fori(1, (STEPS - 3) // 2) as i:
                        for j in range(2):
                            n, s = b + 2 + 3 * j, 1 + j
                            full_in(n, 0, f + s, i)
                            full_in(n + 1, 1, f + s, i)
                            step_out(n + 2, (s - 1) % 2, e + s, False, i)
                    n = b + 2 + 3 * (STEPS - 3)
                    for s in (STEPS - 2, STEPS - 1):
                        full_in(n, 0, f + s)
                        full_in(n + 1, 1, f + s)
                        n += 2
                    if k == 0:
                        pe.wait_ge(mix0_landed, 16 * 7)
                        bank = small_bank("taps")
                        for c in range(CT):
                            mm = pe.transpose(bank[:, c * TAPS:(c + 1) * TAPS], tap_rows[:, c * P:(c + 1) * P],
                                              ident[0:TAPS, 0:TAPS])
                        mm.then_inc(small_full, 1)
                        pe.transpose(small_bank("columns")[:, 0:5 * CT], col_rows, ident[0:5 * CT, 0:5 * CT])\
                            .then_inc(small_full, 1)
                    tail(k, [(n + a, 2 * a) for a in range(3)],
                         lambda a: pe.wait_ge(h_done, e + STEPS - 2 + a))
                elif kind == "mix0":
                    first_pair(k, f)
                    slab_in(b + 2, open_bank(b + 2, 0, f + 1), lambda: hidden(k, f)).then_inc(slab_used, 1)
                    full_in(b + 3, 1, f + 1)
                    for a in range(2):
                        bank = open_bank(b + 4 + a, a, f + 2)
                        for t in range(TT):
                            mm = slab_in_rows(b + 4 + a, bank, t)
                        mm.then_inc(slab_used, 1)

                    def convolve(lo, hi):
                        for m in range(lo, hi):
                            c, q = pe_taps[m]
                            pe.wait_ge(tap_built, m + 1)
                            pe.matmul(ga[:, 0, :] if c == CT - 1 else ub[:, 1, :], tap_diag(m),
                                      conv_in[:, c, q:q + T], start=m in (0, TAPS),
                                      stop=q == TAPS - 1).then_inc(tap_used, 1)

                    pe.wait_ge(ub_free, f + 2)
                    pe.wait_ge(ga_free, f + 3)
                    convolve(0, DIAGS)
                    pe.wait_ge(window_done, 2)
                    pe.wait_ge(ub_free, f + 3)
                    for j in range(2):
                        bank = small_bank(("pooled", j))
                        for a in range(2):
                            g = 2 * j + a
                            pe.matmul(bank[:, a * T:(a + 1) * T], u[:, 0, g * P:(g + 1) * P],
                                      window[:, g, 0:2, :].rearrange("p b t -> p (b t)"), start=True, stop=False)
                            mm = pe.matmul(bank[:, a * T + P:(a + 1) * T], u[:, 1, g * P:(g + 1) * P],
                                           window[:, g, 2, :], start=False, stop=True)
                        mm.then_inc(small_full, 1)
                    convolve(DIAGS, TAPS - 8)
                    for j in range(2):
                        bank = small_bank(("pool", j))
                        pe.wait_ge(small_free, small[("pooled", j)] + 1)
                        for a in range(2):
                            g = 2 * j + a
                            mm = pe.matmul(bank[:, a * T:(a + 1) * T], pw[:, g, :], pooled[:, g, :],
                                           start=True, stop=True)
                        mm.then_inc(small_full, 1)
                    convolve(TAPS - 8, len(pe_taps))
                    slab_ready(b + 6)
                    pe.wait_ge(mix_ready, 1)
                    slab_out(b + 6, 0, 0, True, False)
                    pe.wait_ge(ga_free, f + 4)
                    pe.wait_ge(conv_step, (CT - 1) * TAPS - SHARED + 1)
                    for c in range(CT):
                        mm = pe.matmul(ub[:, 0, :], avg[:, :], y[:, c, :], start=c == 0, stop=c == CT - 1)
                    mm.then_inc(mean_full, 1)
                    slab_out(b + 6, 1, 0, True, False).then_inc(slab_used, 1)
                    bank = small_bank("var")
                    for t in range(TT):
                        for c in range(CT):
                            if t == 0 and c % 2 == 0:
                                pe.wait_ge(sq_ready, c // 2 + 1)
                            mm = pe.matmul(bank[:, t:t + 1], sq[:, c, t * P:(t + 1) * P], avg[:, 0:1],
                                           start=c == 0, stop=c == CT - 1)
                    mm.then_inc(small_full, 1)

                    def spread():
                        bank = small_bank("spread")
                        pe.wait_ge(diag_ready, TT)
                        pe.matmul(bank[:, 0:T], ones[:, :], diag, start=True, stop=True).then_inc(small_full, 1)

                    slab_ready(b + 7)
                    pe.wait_ge(mix_ready, 2)
                    slab_out(b + 7, 0, 2, False, False, spread)
                    slab_out(b + 7, 1, 2, False, False).then_inc(slab_used, 1)
                    tail(k, [(b + 8, 4), (b + 9, 6)], lambda a: pe.wait_ge(mix_ready, 3 + a))
                else:
                    first_pair(k, f)
                    for j in range(2, 4):
                        bank, free = ((ga, ga_free), (ub, ub_free))[j % 2]
                        slab_ready(b + j)
                        pe.wait_ge(free, f + 1)
                        for t in range(TT):
                            mm = slab_in_rows(b + j, bank, t)
                        mm.then_inc(slab_used, 1)
                    full_in(b + 4, 0, f + 2)
                    full_in(b + 5, 1, f + 2)
                    for j in range(2):
                        bank = small_bank(("spatial_w", j))
                        pe.wait_ge(mask_ready, 1)
                        for a in range(4):
                            mm = pe.transpose(bank[:, a * P:(a + 1) * P], spatial_w[:, 4 * j + a, :], ident[:, :])
                        mm.then_inc(small_full, 1)
                    full_in(b + 6, 0, f + 3)

                    def spatial(j):
                        bank = small_bank(("spatial", j))
                        pe.wait_ge(small_free, small[("spatial_w", 1)] + 1)
                        for a in range(2):
                            for t in range(TT):
                                h = 2 * j + a
                                pe.wait_ge(v_ready, t + 1)
                                o = (a * TT + t) * P
                                mm = pe.matmul(bank[:, o:o + P], xs[:, t, h * P:(h + 1) * P], spatial_wT[:, h, :],
                                               start=True, stop=True)
                        mm.then_inc(small_full, 1)

                    spatial(0)
                    spatial(1)
                    full_in(b + 7, 1, f + 3)
                    spatial(2)
                    spatial(3)
                    tail(k, [(b + 8 + j, 2 * j) for j in range(4)], lambda a: pe.wait_ge(gu_done, a + 1), b + 8)


_INS = ['x', 'ffn1_norm', 'ffn1_w_in', 'ffn1_w_out', 'mix_norm', 'ffn2_norm', 'ffn2_w_in', 'ffn2_w_out',
        'ab_w_in', 'pool_w', 'pool_b', 'pool_scale', 'conv_w', 'conv_b', 'conv_ln_g', 'conv_ln_b', 'ab_w_out',
        'sgu_w_in', 'sgu_ln_g', 'sgu_ln_b', 'sgu_w', 'sgu_b', 'sgu_w_out', 'final_norm']
_OUTS = [((1, 256, 1024), 'float32')]


def kernel(**inputs):
    import numpy as _np
    import concourse.bacc as _bacc
    from concourse import mybir as _mybir
    from concourse.bass_utils import run_bass_kernel_spmd as _run

    nc = _bacc.Bacc("TRN2", target_bir_lowering=False, num_devices=1)
    arrays, args = {}, []
    for name in _INS:
        a = _np.ascontiguousarray(inputs[name])
        arrays[f"in_{name}_dram"] = a
        args.append(nc.dram_tensor(f"in_{name}_dram", a.shape, _mybir.dt.from_np(a.dtype), kind="ExternalInput").ap())
    for i, (shape, dtype) in enumerate(_OUTS):
        dt = _mybir.dt.from_np(_np.dtype(dtype))
        args.append(nc.dram_tensor(f"out_{i}_dram", shape, dt, kind="ExternalOutput").ap())
    hybrid_trunk(nc, *args)
    r = _run(nc, [arrays], core_ids=[0])
    got = tuple(r.results[0][f"out_{i}_dram"] for i in range(len(_OUTS)))
    return got[0]
```
